# Optimizing a Trainium2 kernel written in Bass

```python
import math
import jax, jax.numpy as jnp
from jax import lax
import numpy as np

D_MODEL = 1024
BATCH = 1
SEQ = 1024
DEPTH = 1
DEC_BATCH = 8
DEC_SEQ = 8
PAST_LEN = 1024
PAGE_SIZE = 128

N_META = 16
EPS = 1e-6
ROPE_THETA = 10000.0
MLA_HEADS = 8
Q_LORA = 256
KV_LORA = 128
NOPE_DIM = 64
ROPE_DIM = 32
V_DIM = 64
MLA_SCALE = 1.0 / math.sqrt(NOPE_DIM + ROPE_DIM)
Q_BLOCK = 128
RET_HEADS = 8
RET_DK = 64
RET_DV = 64
RET_CHUNK = 128
MIX_WIDTH = MLA_HEADS * V_DIM + RET_HEADS * RET_DV
IN_WIDTH = Q_LORA + KV_LORA + ROPE_DIM + 3 * RET_HEADS * RET_DK + RET_HEADS * RET_DV
PEER_HEADS = 8
N_KEYS = 128
N_EXPERTS = N_KEYS * N_KEYS
PEER_KEY_DIM = 128
PEER_TOPK = 16
PEER_BLOCK = 128

kernel_name = 'hymba_mla_retention_peer_step'

def rmsnorm(x, g):
    xf = x.astype(jnp.float32)
    y = xf * lax.rsqrt(jnp.mean(xf * xf, axis=-1, keepdims=True) + EPS)
    return (y * g.astype(jnp.float32)).astype(x.dtype)

def head_norm(x):
    xf = x.astype(jnp.float32)
    y = xf * lax.rsqrt(jnp.mean(xf * xf, axis=-1, keepdims=True) + EPS)
    return y.astype(x.dtype)

def rope(x, pos):
    half = x.shape[-1] // 2
    inv = ROPE_THETA ** (-jnp.arange(half, dtype=jnp.float32) / half)
    ang = pos.astype(jnp.float32)[:, None] * inv[None, :]
    shp = (pos.shape[0],) + (1,) * (x.ndim - 3) + (half,)
    cos = jnp.cos(ang).reshape(shp).astype(x.dtype)
    sin = jnp.sin(ang).reshape(shp).astype(x.dtype)
    x1, x2 = x[..., :half], x[..., half:]
    return jnp.concatenate([x1 * cos - x2 * sin, x1 * sin + x2 * cos], axis=-1)

def in_split_points():
    widths = (Q_LORA, KV_LORA, ROPE_DIM, RET_HEADS * RET_DK, RET_HEADS * RET_DK, RET_HEADS * RET_DV)
    pts, acc = [], 0
    for w in widths:
        acc += w
        pts.append(acc)
    return pts

def mixer_inputs(h, pos, w_in, g_q, w_uq, g_kv, w_uk):
    b, l, _ = h.shape
    c_q, c_kv, k_r, r_q, r_k, r_v, r_g = jnp.split(h @ w_in, in_split_points(), axis=-1)
    q = jnp.einsum('blc,chd->blhd', rmsnorm(c_q, g_q), w_uq)
    q_rope = rope(q[..., NOPE_DIM:], pos)
    q_lat = jnp.einsum('blhd,chd->blhc', q[..., :NOPE_DIM], w_uk)
    ckv = rmsnorm(c_kv, g_kv)
    krope = rope(k_r, pos)
    rq = rope(r_q.reshape(b, l, RET_HEADS, RET_DK), pos)
    rk = rope(r_k.reshape(b, l, RET_HEADS, RET_DK), pos) * (RET_DK ** -0.5)
    rv = r_v.reshape(b, l, RET_HEADS, RET_DV)
    return q_lat, q_rope, ckv, krope, rq, rk, rv, r_g

def mla_attend(q_lat, q_rope, ckv, krope, q_pos, k_pos):
    s = jnp.einsum('bqhc,bkc->bhqk', q_lat, ckv) + jnp.einsum('bqhr,bkr->bhqk', q_rope, krope)
    s = s.astype(jnp.float32) * MLA_SCALE
    s = jnp.where(k_pos[None, :] <= q_pos[:, None], s, -jnp.inf)
    p = jax.nn.softmax(s, axis=-1).astype(ckv.dtype)
    return jnp.einsum('bhqk,bkc->bqhc', p, ckv)

def mla_prompt(q_lat, q_rope, ckv, krope):
    b, l = q_lat.shape[:2]
    nb = -(-l // Q_BLOCK)
    lp = nb * Q_BLOCK
    pad_len = lambda a: jnp.pad(a, [(0, 0), (0, lp - l)] + [(0, 0)] * (a.ndim - 2))
    q_lat, q_rope, ckv, krope = pad_len(q_lat), pad_len(q_rope), pad_len(ckv), pad_len(krope)
    k_pos = jnp.arange(lp)

    def to_blocks(a):
        return jnp.moveaxis(a.reshape((b, nb, Q_BLOCK) + a.shape[2:]), 1, 0)

    def blk(args):
        qb, qrb, qp = args
        return mla_attend(qb, qrb, ckv, krope, qp, k_pos)

    out = lax.map(blk, (to_blocks(q_lat), to_blocks(q_rope), k_pos.reshape(nb, Q_BLOCK)))
    out = jnp.moveaxis(out, 0, 1).reshape((b, lp) + out.shape[3:])
    return out[:, :l]

def ret_chunk(s, q, k, v):
    c = q.shape[1]
    log_g = jnp.log(1.0 - 2.0 ** (-5.0 - jnp.arange(RET_HEADS, dtype=jnp.float32)))
    i = jnp.arange(c, dtype=jnp.float32)
    rel = i[:, None] - i[None, :]
    dmat = jnp.where(rel >= 0, jnp.exp(log_g[:, None, None] * jnp.maximum(rel, 0.0)), 0.0).astype(q.dtype)
    inner = jnp.einsum('bihd,bjhd->bhij', q, k) * dmat
    o = jnp.einsum('bhij,bjhe->bihe', inner, v)
    cross = jnp.exp(log_g[None, :] * (i[:, None] + 1.0)).astype(q.dtype)
    o = o + jnp.einsum('bihd,bhde->bihe', q, s) * cross[None, :, :, None]
    kdec = jnp.exp(log_g[None, :] * (c - 1.0 - i)[:, None]).astype(q.dtype)
    s_new = s * jnp.exp(log_g * c).astype(s.dtype)[None, :, None, None] \
        + jnp.einsum('bjhd,bjhe->bhde', k * kdec[None, :, :, None], v).astype(s.dtype)
    return s_new, o

def retention_prompt(q, k, v):
    b = q.shape[0]
    s0 = jnp.zeros((b, RET_HEADS, RET_DK, RET_DV), q.dtype)
    s_meta, o_meta = ret_chunk(s0, q[:, :N_META], k[:, :N_META], v[:, :N_META])
    nc = (q.shape[1] - N_META) // RET_CHUNK

    def chunks(a):
        return jnp.moveaxis(a[:, N_META:].reshape(b, nc, RET_CHUNK, RET_HEADS, a.shape[-1]), 1, 0)

    s_fin, o = lax.scan(lambda st, qkv: ret_chunk(st, qkv[0], qkv[1], qkv[2]), s_meta,
                        (chunks(q), chunks(k), chunks(v)))
    o = jnp.moveaxis(o, 0, 1).reshape(b, nc * RET_CHUNK, RET_HEADS, RET_DV)
    return s_fin, jnp.concatenate([o_meta, o], axis=1)

def mixer_output(lat, ro, r_g, w_uv, w_out):
    b, l = lat.shape[:2]
    mla = jnp.einsum('blhc,chd->blhd', lat, w_uv).reshape(b, l, MLA_HEADS * V_DIM)
    ret = head_norm(ro).reshape(b, l, RET_HEADS * RET_DV) * jax.nn.silu(r_g)
    return jnp.concatenate([mla, ret], axis=-1) @ w_out

def peer_ffn(h, w_q, sub_keys, u_tab, v_tab):
    b, l, d = h.shape
    t = b * l
    nb = -(-t // PEER_BLOCK)
    hf = jnp.pad(h.reshape(t, d), ((0, nb * PEER_BLOCK - t), (0, 0))).reshape(nb, PEER_BLOCK, d)

    def blk(hb):
        q = (hb @ w_q).reshape(PEER_BLOCK, PEER_HEADS, 2, PEER_KEY_DIM // 2)
        sc = jnp.einsum('thpd,hpnd->thpn', q, sub_keys).astype(jnp.float32)
        s1, i1 = lax.top_k(sc[:, :, 0], PEER_TOPK)
        s2, i2 = lax.top_k(sc[:, :, 1], PEER_TOPK)
        cand = (s1[..., :, None] + s2[..., None, :]).reshape(PEER_BLOCK, PEER_HEADS, PEER_TOPK * PEER_TOPK)
        top_s, ci = lax.top_k(cand, PEER_TOPK)
        e = jnp.take_along_axis(i1, ci // PEER_TOPK, axis=-1) * N_KEYS \
            + jnp.take_along_axis(i2, ci % PEER_TOPK, axis=-1)
        gate = jax.nn.softmax(top_s, axis=-1).astype(hb.dtype)
        act = jax.nn.gelu(jnp.einsum('thkd,td->thk', u_tab[e], hb), approximate=False)
        return jnp.einsum('thk,thkd->td', gate * act, v_tab[e])

    out = lax.map(blk, hf).reshape(nb * PEER_BLOCK, d)[:t]
    return out.reshape(b, l, d)

def setup_inputs(seed: int = 0) -> dict:
    key = jax.random.key(seed)
    ks = jax.random.split(key, 24)
    n_pages = PAST_LEN // PAGE_SIZE
    n_used = DEC_BATCH * n_pages
    n_pool = (n_used * 5) // 4
    nrm = lambda k, shp, sc: jax.random.normal(k, shp, jnp.float32) * sc
    gain = lambda k, n: 1.0 + 0.02 * jax.random.normal(k, (DEPTH, n), jnp.float32)
    page_table = jax.random.permutation(ks[5], n_pool)[:n_used].astype(jnp.int32).reshape(DEC_BATCH, n_pages)
    return {
        'x_prompt': nrm(ks[0], (BATCH, SEQ, D_MODEL), 1.0),
        'x_sample': nrm(ks[1], (DEC_BATCH, DEC_SEQ, D_MODEL), 1.0),
        'cache_ckv': nrm(ks[2], (DEPTH, n_pool, PAGE_SIZE, KV_LORA), 1.0),
        'cache_krope': nrm(ks[3], (DEPTH, n_pool, PAGE_SIZE, ROPE_DIM), 1.0),
        'state_ret': nrm(ks[4], (DEPTH, DEC_BATCH, RET_HEADS, RET_DK, RET_DV), 0.1),
        'page_table': page_table,
        'meta_tokens': nrm(ks[6], (N_META, D_MODEL), 1.0),
        'g_mix': gain(ks[7], D_MODEL),
        'w_in': nrm(ks[8], (DEPTH, D_MODEL, IN_WIDTH), D_MODEL ** -0.5),
        'g_q': gain(ks[9], Q_LORA),
        'w_uq': nrm(ks[10], (DEPTH, Q_LORA, MLA_HEADS, NOPE_DIM + ROPE_DIM), Q_LORA ** -0.5),
        'g_kv': gain(ks[11], KV_LORA),
        'w_uk': nrm(ks[12], (DEPTH, KV_LORA, MLA_HEADS, NOPE_DIM), KV_LORA ** -0.5),
        'w_uv': nrm(ks[13], (DEPTH, KV_LORA, MLA_HEADS, V_DIM), KV_LORA ** -0.5),
        'w_out': nrm(ks[14], (DEPTH, MIX_WIDTH, D_MODEL), MIX_WIDTH ** -0.5),
        'g_ffn': gain(ks[15], D_MODEL),
        'w_query': nrm(ks[16], (DEPTH, D_MODEL, PEER_HEADS * PEER_KEY_DIM), D_MODEL ** -0.5),
        'sub_keys': nrm(ks[17], (DEPTH, PEER_HEADS, 2, N_KEYS, PEER_KEY_DIM // 2), (PEER_KEY_DIM // 2) ** -0.5),
        'u_experts': nrm(ks[18], (DEPTH, N_EXPERTS, D_MODEL), D_MODEL ** -0.5),
        'v_experts': nrm(ks[19], (DEPTH, N_EXPERTS, D_MODEL), 0.5),
        'g_final': 1.0 + 0.02 * jax.random.normal(ks[20], (D_MODEL,), jnp.float32),
    }

def reference(x_prompt, x_sample, cache_ckv, cache_krope, state_ret, page_table, meta_tokens,
              g_mix, w_in, g_q, w_uq, g_kv, w_uk, w_uv, w_out, g_ffn, w_query, sub_keys,
              u_experts, v_experts, g_final):
    b = x_prompt.shape[0]
    db, n_pages = page_table.shape
    past = n_pages * PAGE_SIZE
    dec = x_sample.shape[1]
    lp = N_META + x_prompt.shape[1]
    pos_p = jnp.arange(lp)
    pos_s = past + jnp.arange(dec)
    k_pos_s = jnp.arange(past + dec)

    meta = jnp.broadcast_to(meta_tokens.astype(x_prompt.dtype)[None], (b, N_META, D_MODEL))
    xp = jnp.concatenate([meta, x_prompt], axis=1)
    xs = x_sample
    ckv_p_l, kr_p_l, ckv_s_l, kr_s_l, rs_p_l, rs_s_l = [], [], [], [], [], []

    for l in range(DEPTH):
        q_lat, q_rope, ckv, krope, rq, rk, rv, rg = mixer_inputs(
            rmsnorm(xp, g_mix[l]), pos_p, w_in[l], g_q[l], w_uq[l], g_kv[l], w_uk[l])
        lat = mla_prompt(q_lat, q_rope, ckv, krope)
        s_p, ro = retention_prompt(rq, rk, rv)
        xp = xp + mixer_output(lat, ro, rg, w_uv[l], w_out[l])
        xp = xp + peer_ffn(rmsnorm(xp, g_ffn[l]), w_query[l], sub_keys[l], u_experts[l], v_experts[l])
        ckv_p_l.append(ckv)
        kr_p_l.append(krope)
        rs_p_l.append(s_p)

        q_lat_s, q_rope_s, ckv_s, krope_s, rq_s, rk_s, rv_s, rg_s = mixer_inputs(
            rmsnorm(xs, g_mix[l]), pos_s, w_in[l], g_q[l], w_uq[l], g_kv[l], w_uk[l])
        ckv_all = jnp.concatenate(
            [cache_ckv[l][page_table].reshape(db, past, KV_LORA).astype(ckv_s.dtype), ckv_s], axis=1)
        kr_all = jnp.concatenate(
            [cache_krope[l][page_table].reshape(db, past, ROPE_DIM).astype(krope_s.dtype), krope_s], axis=1)
        lat_s = mla_attend(q_lat_s, q_rope_s, ckv_all, kr_all, pos_s, k_pos_s)
        s_s, ro_s = ret_chunk(state_ret[l].astype(rq_s.dtype), rq_s, rk_s, rv_s)
        xs = xs + mixer_output(lat_s, ro_s, rg_s, w_uv[l], w_out[l])
        xs = xs + peer_ffn(rmsnorm(xs, g_ffn[l]), w_query[l], sub_keys[l], u_experts[l], v_experts[l])
        ckv_s_l.append(ckv_s)
        kr_s_l.append(krope_s)
        rs_s_l.append(s_s)

    y_prompt = rmsnorm(xp, g_final)[:, N_META:]
    y_sample = rmsnorm(xs, g_final)
    new_ckv_prompt = jnp.stack(ckv_p_l, axis=0)
    new_krope_prompt = jnp.stack(kr_p_l, axis=0)
    new_ckv_sample = jnp.stack(ckv_s_l, axis=0)
    new_krope_sample = jnp.stack(kr_s_l, axis=0)
    new_ret_prompt = jnp.stack(rs_p_l, axis=0)
    new_ret_sample = jnp.stack(rs_s_l, axis=0)
    return (y_prompt, y_sample, new_ckv_prompt, new_krope_prompt, new_ckv_sample, new_krope_sample,
            new_ret_prompt, new_ret_sample)


_drawn_inputs = setup_inputs


def setup_inputs(seed=0):
    import zlib

    import numpy as np

    out = dict(_drawn_inputs(seed))
    spreads = {}
    factors = {'g_q': 5.784, 'g_final': 2.935}
    for name, (base, spread) in spreads.items():
        noise = np.random.default_rng([zlib.crc32(name.encode()), seed]).standard_normal(out[name].shape)
        drawn = base * np.exp(spread * noise) if base else spread * noise
        out[name] = __import__('jax').numpy.asarray(drawn.astype(out[name].dtype))
    for name, factor in factors.items():
        out[name] = (out[name] * factor).astype(out[name].dtype)
    return out
```

```python
from contextlib import ExitStack

import numpy as np
import concourse.bass as bass
from concourse import mybir

F32 = mybir.dt.float32
BF16 = mybir.dt.bfloat16
U32 = mybir.dt.uint32
U16 = mybir.dt.uint16
I32 = mybir.dt.int32
ACT = mybir.ActivationFunctionType
ALU = mybir.AluOpType
AX = mybir.AxisListType.X

P = 128
D = 1024
NCH = D // P
SEQ = 1024
N_META = 16
NTILE = SEQ // P
DEC_B, DEC_T = 8, 8
NSMP = DEC_B * DEC_T
H = 8
Q_LORA, KV, NOPE, ROPE, VD = 256, 128, 64, 32, 64
IN_W = Q_LORA + KV + ROPE + 4 * H * 64
C_KV, C_KR, C_RQ, C_RK, C_RV, C_RG = 256, 384, 416, 928, 1440, 1952
SCALE = (NOPE + ROPE) ** -0.5
EPS = 1e-6
NKEY = SEQ + P
NKC = NKEY // P
PAGES = 8
TOPK = 16
NEG = -3.0e38
RING = 4
GRP = 8
PAIRS = [(a, b) for a in range(TOPK) for b in range(TOPK) if (a + 1) * (b + 1) <= TOPK]
NPAIR = len(PAIRS)

STRETCHES = ("first", "second", "loop", "last")
LOOP0 = 2


def build(nc, A, counts, marks):
    new_counts, new_marks = {}, {}
    ctx = ExitStack()
    with ctx:
        def sb(name, shape, dt=F32):
            return ctx.enter_context(nc.sbuf_tensor(name, shape, dt))

        def sem(name):
            return ctx.enter_context(nc.semaphore(name))

        w_in = sb("w_in", [P, NCH, IN_W])
        w_uq = sb("w_uq", [P, 2, H * 96])
        ukT = sb("ukT", [P, 4, KV])
        w_uv = sb("w_uv", [P, H * VD])
        keysT = sb("keysT", [P, H, P])
        gains = sb("gains", [33, D])
        gcol = sb("gcol", [P, NCH + 2])
        gkv = sb("gkv", [P, KV])
        ident = sb("ident", [P, P])
        fold = sb("fold", [P, P])
        ones = sb("ones", [33, P])
        dmat = sb("dmat", [P, H, P])
        rowc = sb("rowc", [P, 29])
        trig = sb("trig", [P, 64])
        iota = sb("iota", [P, NPAIR])
        mask16 = sb("mask16", [P, NKEY], U16)
        ckvT = sb("ckvT", [P, NKEY])
        krT = sb("krT", [ROPE, NKEY])
        ckvR = sb("ckvR", [P, NKEY])
        state = sb("state", [P, 4, 64])
        wring = sb("wring", [P, 2, D])
        xa = sb("xa", [P, D])
        ha = sb("ha", [P, D])
        T1 = sb("T1", [P, D])
        B1 = sb("B1", [P, D])
        proj = sb("proj", [P, IN_W])
        PP = sb("PP", [P, NKEY])
        scr = sb("scr", [P, NKEY])
        ckvS = sb("ckvS", [P, KV])
        krS = sb("krS", [P, ROPE])
        small = sb("small", [P, 96])
        latT = sb("latT", [P, P])
        idx_a = sb("idx_a", [P, P], U32)
        gate_a = sb("gate_a", [P, P])
        xr = sb("xr", [P, D])
        hr = sb("hr", [P, D])
        idx_r = sb("idx_r", [P, P], U32)
        gate_r = sb("gate_r", [P, P])
        U = sb("U", [P, RING, D])
        V = sb("V", [P, RING, D])
        diag = sb("diag", [P, RING, P])
        dots = sb("dots", [P, 2, GRP])
        acts = sb("acts", [P, 2, GRP])
        peerv = sb("peerv", [P, 4])
        epsc = sb("epsc", [P, 1])
        PS = ctx.enter_context(nc.psum_tensor("PS", [P, 8 * 512], F32))
        Y = PS[:, 0:1024]
        PA = PS[:, 1024:2560]
        PB = PS[:, 2560:4096]

        def apart(h):
            return 4 * (h % 2) + h // 2

        def cross_at(h):
            return 512 + 512 * (h % 2) + 64 * (h // 2)

        gq = gcol[:, NCH:NCH + 2]
        onehot, crossc, kdecc, gchunk = rowc[:, 0:9], rowc[:, 9:17], rowc[:, 17:25], rowc[:, 25:29]
        cat = ha
        cachev = U[:, 0, :]
        kcT = U[:, 1, :]
        krcT = U[:, 2, :]
        krc = U[:, 3, :]
        latS = U[:, 3, 512:1024]
        sst = V[:, 0:2, :].rearrange("p a (b c e) -> p (a b) c e", b=4, c=4)
        mask = mask16[:].bitcast(BF16)
        newm = mask[0:64, 0:248]
        kdb = U[:, 1, :]
        trig2 = trig[:].rearrange("p (s f two) -> p s f two", s=2, two=2)

        names = ["dve", "act", "pe", "pool"] + [f"gu{i}" for i in range(RING)] + [f"gv{i}" for i in range(RING)] + \
            ["w0", "w1", "x_in", "ld_id", "const", "kv_out", "y_out", "ld_w", "st_in", "st_out", "pg"] + \
            [f"win{n}" for n in range(5)] + ["tick_dve", "tick_pool", "tick_sp"] + \
            ["cache0", "cache1", "dup"]
        S = {n: sem({"dve": "dve_done", "act": "act_done", "pe": "pe_done", "pool": "pool_done"}.get(n, n))
             for n in names}

        dve_done, act_done, pe_done, pool_done = S["dve"], S["act"], S["pe"], S["pool"]

        def start(s, st, T):
            c = lambda x: counts.get((s, x), 0)
            if st == "first":
                return 0
            if st == "second":
                return c("first")
            if st == "loop":
                return T * c("loop") + (c("first") + c("second") - LOOP0 * c("loop"))
            return c("first") + c("second") + (NTILE + 1 - LOOP0) * c("loop")

        class Counter:
            def __init__(self, eng, own):
                self.eng, self.own, self.st, self.T = eng, own, "first", 0

            def count(self, name=None, s=None, by=1):
                s = s or self.own
                new_counts[(s, self.st)] = new_counts.get((s, self.st), 0) + by
                if name is not None:
                    assert (s, self.st, name) not in new_marks, (s, self.st, name)
                    new_marks[(s, self.st, name)] = new_counts[(s, self.st)]
                return by

            def at(self, s, name):
                assert not marks or (s, self.st, name) in marks, (s, self.st, name)
                return start(s, self.st, self.T) + marks.get((s, self.st, name), 1)

            def here(self):
                return start(self.own, self.st, self.T) + new_counts[(self.own, self.st)]

            def meet(self, st, T):
                self.st, self.T = st, T
                if st != "first":
                    for s in ("dve", "act", "pe", "pool"):
                        self.eng.wait_ge(S[s], start(s, st, T))
                        if self.own in ("sp", "pool"):
                            self.eng.sem_inc(S["tick_" + self.own], 1)

        MIX = ["norm1", "proj", "kv", "ret1", "ret2", "q1"] + [f"att{h}" for h in range(H)] + \
            ["out", "norm2", "query", "top1", "top2", "top3"]

        def plan(st):
            if st == "first":
                return [(m, None) for m in MIX]
            ng = (NSMP if st == "second" else P) // GRP + 1
            if st == "last":
                return [(None, g) for g in range(ng)]
            out, g = [], 0
            for n, m in enumerate(MIX):
                out.append((m, None))
                while g < ng and (g + 1) * len(MIX) <= (n + 1) * ng + len(MIX) // 2:
                    out.append((None, g))
                    g += 1
            out += [(None, x) for x in range(g, ng)]
            return out

        def nslots(st):
            return NSMP if st == "second" else P

        def run(eng_counter, steps, peer, tail, eng):
            c = eng_counter

            def stretch(st, T):
                c.meet(st, T)
                if "begin" in steps:
                    steps["begin"](st, T)
                for m, g in plan(st):
                    if m is not None:
                        key = m[:3] if m.startswith("att") else m
                        if key in steps:
                            (steps[key](st, T, int(m[3:])) if key == "att" else steps[key](st, T))
                    elif peer is not None:
                        peer(st, T, g)
                tail(st, T)

            stretch("first", 0)
            stretch("second", 1)
            with eng.Fori(LOOP0, NTILE + 1) as T:
                stretch("loop", T)
            stretch("last", NTILE + 1)

        block = ctx.enter_context(nc.Block())

        @block.sync
        def _(e):
            c = Counter(e, "sp")

            def dma(out, in_, s, name):
                e.dma_start(out, in_).then_inc(S[s], c.count(name, s, 16))

            def norm1(st, T):
                if st == "first":
                    e.wait_ge(pool_done, c.at("pool", "x cleared"))
                    e.sem_inc(S["tick_sp"], 1)
                    dma(xa[0:NSMP, :], A["x_sample"].rearrange("b t d -> (b t) d"), "x_in", "xs")
                    dma(xa[NSMP:NSMP + N_META, :], A["meta_tokens"], "x_in", "x")
                    dma(ident[:], A["c_ident"], "ld_id", "i")
                    dma(gcol[:], A["t_gcol"], "ld_id", "gq")
                    src = A["w_in"].rearrange("o (c p) n -> p (o c) n", p=P)
                    for n in range(5):
                        dma(w_in[:, :, 512 * n:min(512 * n + 512, IN_W)], src[:, :, 512 * n:min(512 * n + 512, IN_W)],
                            f"win{n}", "w")
                    dma(gkv[:], A["g_kv"].rearrange("o k -> (o k)").partition_broadcast(P), "const", "gkv")
                    dma(trig[:], A["c_trig"][0:P, :], "const", "trig")
                    dma(rowc[:], A["c_row0"], "const", "rowc")
                    dma(dmat[:], A["c_dmat0"], "const", "dmat")
                    dma(fold[:], A["c_fold"], "const", "fold")
                    dma(iota[:], A["c_iota"], "const", "iota")
                    dma(mask16[0:64, 0:248], A["c_new"], "const", "newm")
                    dma(gains[0:1, :], A["g_ffn"], "const", "gffn")
                    dma(gains[32:33, :], A["g_final"].rearrange("(o k) -> o k", o=1), "const", "all")
                    st_in = A["state_ret"].rearrange("o b (c a) d e -> (o a) d b c e", a=2)
                    for a in range(2):
                        for b in range(DEC_B):
                            dma(sst[64 * a:64 * a + 64, b, :, :], st_in[a, :, b, :, :], "st_in", f"s{a}{b}")
                    dma(w_uq[:], A["w_uq"].rearrange("o (c p) h d -> p (o c) (h d)", p=P), "ld_w", "w_uq")
                    dma(ukT[:], A["t_uk"], "ld_w", "ukT")
                    dma(w_uv[:], A["w_uv"].rearrange("o c h d -> c (o h d)"), "ld_w", "w_uv")
                    dma(keysT[:], A["t_keys"], "ld_w", "all")
                else:
                    row = (T - 1) * P
                    dma(xa[:], A["x_prompt"].rearrange("b t d -> (b t) d")[bass.ds(row, P), :], "x_in", "x")
                    dma(trig[:], A["c_trig"][bass.ds(T * P, P), :], "const", "trig")
                    if st == "second":
                        dma(rowc[:], A["c_row1"], "const", "rowc")
                        dma(dmat[:], A["c_dmat1"], "const", "dmat")
                    dma(mask16[:], A["c_mask"][bass.ds(T * P, P), :], "const", "all")

            def kv(st, T):
                e.wait_ge(dve_done, c.at("dve", "krope"))
                e.sem_inc(S["tick_sp"], 1)
                if st == "first":
                    dma(A["o_ckv_s"], ckvS[0:NSMP, :], "kv_out", "a")
                    dma(A["o_kr_s"], krS[0:NSMP, :], "kv_out", "b")
                    dma(A["o_ckv_p"][0:N_META, :], ckvS[NSMP:NSMP + N_META, :], "kv_out", "c")
                    dma(A["o_kr_p"][0:N_META, :], krS[NSMP:NSMP + N_META, :], "kv_out", "stored")
                else:
                    row = (T - 1) * P + N_META
                    dma(A["o_ckv_p"][bass.ds(row, P), :], ckvS[:], "kv_out", "a")
                    dma(A["o_kr_p"][bass.ds(row, P), :], krS[:], "kv_out", "stored")

            def ret2(st, T):
                if st == "first":
                    e.wait_ge(dve_done, c.at("dve", "states"))
                    e.sem_inc(S["tick_sp"], 1)
                    out = A["o_rs"].rearrange("b (c a) d e -> a d b c e", a=2)
                    for a in range(2):
                        for b in range(DEC_B):
                            dma(out[a, :, b, :, :], sst[64 * a:64 * a + 64, b, :, :], "st_out", f"o{a}{b}")

            def stream(st, which):
                w = A[which].rearrange("o k n -> (o k) n")
                for k in range(NCH):
                    q = ("o" if which == "w_out" else "q") + str(k)
                    if which == "w_query" or k >= 2:
                        prev = ("o" if (which == "w_out" or k < 2) else "q") + str((k - 2) % NCH)
                        e.wait_ge(pe_done, c.at("pe", "used " + prev))
                        e.sem_inc(S["tick_sp"], 1)
                    dma(wring[:, k % 2, :], w[k * P:(k + 1) * P, :], f"w{k % 2}", q)

            def out(st, T):
                stream(st, "w_out")
                if st == "first":
                    e.wait_ge(dve_done, c.at("dve", "residual"))
                    e.sem_inc(S["tick_sp"], 1)
                    dma(xa[NSMP:P, :], xa[0:NSMP, :], "dup", "dup")

            def query(st, T):
                stream(st, "w_query")

            def tail(st, T):
                if st == "first":
                    return
                e.wait_ge(dve_done, c.at("dve", "y"))
                e.sem_inc(S["tick_sp"], 1)
                if st == "second":
                    dma(A["o_ys"], xr[0:NSMP, :], "y_out", "y")
                else:
                    dma(A["o_yp"][bass.ds((T - 2) * P, P) if st == "loop" else slice(SEQ - P, SEQ), :], xr[:],
                        "y_out", "y")
                if st == "last":
                    st_out = A["o_rp"].rearrange("(c a) d e -> a d c e", a=2)
                    for a in range(2):
                        dma(st_out[a], state[64 * a:64 * a + 64, :, :], "st_out", f"rp{a}")
                    for s in ("kv_out", "y_out", "st_out"):
                        e.wait_ge(S[s], start(s, "last", 0) + new_counts.get((s, "last"), 0))

            run(c, dict(norm1=norm1, kv=kv, ret2=ret2, out=out, query=query), None, tail, e)

        @block.gpsimd
        def _(e):
            c = Counter(e, "pool")

            def gather(dst, table, index, s, name):
                e.indirect_dma_start(dst, None, table, bass.IndirectOffsetOnAxis(ap=index, axis=0)).then_inc(S[s], c.count(name, s, 16))

            def begin(st, T):
                if st != "first":
                    return
                e.memset(epsc[:], EPS).then_inc(pool_done, c.count())
                e.memset(xa[:], 0.0).then_inc(pool_done, c.count("x cleared"))
                e.memset(ckvR[:], 0.0).then_inc(pool_done, c.count())
                e.memset(ckvT[:], 0.0).then_inc(pool_done, c.count())
                e.memset(krT[:], 0.0).then_inc(pool_done, c.count())
                e.memset(ha[:], 0.0).then_inc(pool_done, c.count())
                e.memset(ones[:], 1.0).then_inc(pool_done, c.count("cleared"))
                pt = A["page_table"].rearrange("b g -> (b g)").partition_broadcast(P)
                e.dma_start(idx_r[:, 64:128].bitcast(I32), pt).then_inc(S["pg"], c.count("pages", "pg", 16))
                e.iota(small[:, 90:91].bitcast(I32), [[0, 1]], base=0, channel_multiplier=1).then_inc(pool_done, c.count("iota p"))

            def att(st, T, h):
                if st != "first":
                    return
                if h == 0:
                    e.wait_ge(dve_done, c.at("dve", "page rows"))
                if h >= 2:
                    e.wait_ge(pe_done, c.at("pe", f"s keys used {h - 2}"))
                rows = A["cache_ckv"].rearrange("o g k c -> (o g k) c")
                krows = A["cache_krope"].rearrange("o g k c -> (o g k) c")
                dst = cachev if h % 2 == 0 else V[:, 3, :]
                for j in range(PAGES):
                    ix = idx_r[:, h * PAGES + j:h * PAGES + j + 1]
                    gather(dst[:, P * j:P * j + P], rows, ix, f"cache{h % 2}", f"c{h}{j}")
                for j in range(PAGES):
                    ix = idx_r[:, h * PAGES + j:h * PAGES + j + 1]
                    gather(krc[:, 256 * (h % 2) + ROPE * j:256 * (h % 2) + ROPE * j + ROPE], krows, ix,
                           f"cache{h % 2}", f"k{h}{j}")

            ut = A["u_experts"].rearrange("o e d -> (o e) d")
            vt = A["v_experts"].rearrange("o e d -> (o e) d")

            def peer(st, T, g):
                n = nslots(st)
                for j in range(GRP):
                    s = g * GRP + j
                    if s < n:
                        if s >= RING:
                            e.wait_ge(dve_done, c.at("dve", f"u{s - RING}"))
                            e.sem_inc(S["tick_pool"], 1)
                        gather(U[:, s % RING, :], ut, idx_r[:, s:s + 1], f"gu{s % RING}", f"u{s}")
                    s -= GRP
                    if s >= 0:
                        if s >= RING:
                            e.wait_ge(pe_done, c.at("pe", f"v{s - RING}"))
                            e.sem_inc(S["tick_pool"], 1)
                        gather(V[:, s % RING, :], vt, idx_r[:, s:s + 1], f"gv{s % RING}", f"v{s}")

            def tail(st, T):
                e.memset(peerv[:, 3:4], 0.0).then_inc(pool_done, c.count("end"))

            run(c, dict(begin=begin, att=att), peer, tail, e)

        @block.tensor
        def _(e):
            c = Counter(e, "pe")
            mm = e.matmul

            def transposes(src, n, dst, width=P, rows=P):
                for k in range(n):
                    m = e.transpose(dst(k), src(k), ident[0:rows, 0:rows])
                return m

            def norm1(st, T):
                if st == "first":
                    e.wait_ge(S["ld_id"], c.at("ld_id", "gq"))
                e.wait_ge(act_done, c.at("act", "xn"))
                transposes(lambda k: scr[:, P * k:P * k + P], NCH, lambda k: PB[:, P * k:P * k + P]).then_inc(pe_done, c.count("xT"))

            def projection(st, T):
                for n in range(5):
                    lo, hi = 512 * n, min(512 * n + 512, IN_W)
                    if st == "first":
                        e.wait_ge(S[f"win{n}"], c.at(f"win{n}", "w"))
                    if n == 0:
                        e.wait_ge(act_done, c.at("act", "xT0"))
                        e.wait_ge(dve_done, c.at("dve", "xT1"))
                    if n >= 3:
                        e.wait_ge(act_done, c.at("act", f"proj{n - 3}"))
                    for k in range(NCH):
                        m = mm(PA[:, 512 * (n % 3):512 * (n % 3) + hi - lo], T1[:, P * k:P * k + P], w_in[:, k, lo:hi],
                               start=k == 0, stop=k == NCH - 1)
                    m.then_inc(pe_done, c.count(f"proj{n}"))

            def kv(st, T):
                e.wait_ge(dve_done, c.at("dve", "krope"))
                e.wait_ge(act_done, c.at("act", "cqn"))
                e.transpose(PB[:, 0:P], ckvS[:], ident[:])
                e.transpose(PB[0:ROPE, P:2 * P], krS[:], ident[:])
                e.transpose(PB[:, 2 * P:3 * P], B1[:, 0:P], ident[:])
                e.transpose(PB[:, 3 * P:4 * P], B1[:, P:2 * P], ident[:]).then_inc(pe_done, c.count("kvT"))

            def ret1(st, T):
                e.wait_ge(dve_done, c.at("dve", "rope"))
                e.wait_ge(act_done, c.at("act", "cqT"))
                transposes(lambda k: proj[:, C_RQ + P * k:C_RQ + P * k + P], 8,
                                 lambda k: PB[:, 512 + P * k:512 + P * k + P]).then_inc(pe_done, c.count("rT"))
                e.wait_ge(act_done, c.at("act", "rT"))
                for h in range(H):
                    o = 64 * (h % 2)
                    m = mm(PA[:, P * apart(h):P * apart(h) + P], B1[o:o + 64, 512 + P * (h // 2):512 + P * (h // 2) + P],
                           B1[o:o + 64, P * (h // 2):P * (h // 2) + P], start=True, stop=True)
                m.then_inc(pe_done, c.count("inner"))
                if st == "first":
                    e.wait_ge(S["st_in"], c.at("st_in", f"s1{DEC_B - 1}"))
                    for h in range(H):
                        o = 64 * (h % 2)
                        for b in range(DEC_B):
                            at = cross_at(h) + DEC_T * b
                            m = mm(PB[0:64, at:at + DEC_T],
                                   sst[o:o + 64, b, h // 2, :],
                                   B1[o:o + 64, P * (h // 2) + DEC_T * b:P * (h // 2) + DEC_T * b + DEC_T],
                                   start=True, stop=True)
                    m.then_inc(pe_done, c.count("crossT"))
                    e.wait_ge(act_done, c.at("act", "crossT"))
                    for h in range(H):
                        m = e.transpose(PB[0:64, cross_at(h):cross_at(h) + 64], scr[0:64, 64 * h:64 * h + 64],
                                        ident[0:64, 0:64])
                    m.then_inc(pe_done, c.count("cross"))
                else:
                    for h in range(H):
                        o = 64 * (h % 2)
                        m = mm(PB[:, cross_at(h):cross_at(h) + 64], B1[o:o + 64, P * (h // 2):P * (h // 2) + P],
                               state[o:o + 64, h // 2, :], start=True, stop=True)
                    m.then_inc(pe_done, c.count("cross"))
                e.wait_ge(dve_done, c.at("dve", "innerT"))
                for h in range(H):
                    m = mm(PB[:, 64 * h:64 * h + 64], PP[:, P * apart(h):P * apart(h) + P],
                           proj[:, C_RV + 64 * h:C_RV + 64 * h + 64], start=True, stop=True)
                m.then_inc(pe_done, c.count("o1"))

            def ret2(st, T):
                for b in range(DEC_B + 1) if st == "first" else [0]:
                    e.wait_ge(dve_done, c.at("dve", f"kd{b}"))
                    o = 512 * (b % 2)
                    if st != "first":
                        o = 0
                    if b >= 2:
                        e.wait_ge(dve_done, c.at("dve", f"sn{b - 2}"))
                    for q in range(4):
                        m = mm(PA[:, o + P * q:o + P * q + P],
                               (scr[:, 512 + P * q:512 + P * q + P] if st != "first" else
                                kdb[:, 512 * (b % 2) + P * q:512 * (b % 2) + P * q + P]),
                               proj[:, C_RV + P * q:C_RV + P * q + P], start=True, stop=True)
                    m.then_inc(pe_done, c.count(f"su{b}"))

            def q1(st, T):
                if st == "first":
                    e.wait_ge(S["ld_w"], c.at("ld_w", "all"))
                e.wait_ge(dve_done, c.at("dve", "ret"))
                for n in range(2):
                    for k in range(2):
                        m = mm(PA[:, 512 * n:512 * n + 384], ckq(k), w_uq[:, k, 384 * n:384 * n + 384],
                               start=k == 0, stop=k == 1)
                m.then_inc(pe_done, c.count("q"))
                e.wait_ge(act_done, c.at("act", "q rope in"))
                transposes(lambda k: scr[:, P * k:P * k + P], 4, lambda k: PB[:, P * k:P * k + P]).then_inc(pe_done, c.count("qnT"))
                e.wait_ge(dve_done, c.at("dve", "q rope"))
                for h in range(H):
                    m = e.transpose(PB[0:ROPE, 512 + P * h:512 + P * h + P],
                                    scr[:, 512 + ROPE * h:512 + ROPE * h + ROPE], ident[:])
                m.then_inc(pe_done, c.count("qrT"))
                e.wait_ge(act_done, c.at("act", "qnT"))
                for h in range(H):
                    o = 64 * (h % 2)
                    m = mm(PA[:, P * apart(h):P * apart(h) + P], ukT[o:o + 64, h // 2, :],
                           PP[o:o + 64, P * (h // 2):P * (h // 2) + P], start=True, stop=True)
                m.then_inc(pe_done, c.count("qlat"))

            def ckq(k):
                return T1[:, P * k:P * k + P]

            def att_sample(h):
                rows = cachev if h % 2 == 0 else V[:, 3, :]
                kro = 256 * (h % 2)
                e.wait_ge(S["cache" + str(h % 2)], c.at("cache" + str(h % 2), f"k{h}7"))
                if h == 0:
                    e.wait_ge(act_done, c.at("act", "qlat"))
                    e.wait_ge(act_done, c.at("act", "qrT"))
                else:
                    e.wait_ge(dve_done, c.at("dve", f"s pT1 {h - 1}"))
                    e.wait_ge(act_done, c.at("act", f"s lat {h - 1}"))
                transposes(lambda k: rows[:, P * k:P * k + P], 8, lambda k: PB[:, P * k:P * k + P]).then_inc(pe_done, c.count(f"s kT {h}"))
                for k in range(PAGES):
                    m = e.transpose(PA[0:ROPE, P * k:P * k + P], krc[:, kro + ROPE * k:kro + ROPE * k + ROPE], ident[:])
                m.then_inc(pe_done, c.count(f"s krT {h}"))
                e.wait_ge(act_done, c.at("act", f"s kT {h}"))
                e.wait_ge(dve_done, c.at("dve", f"s krT {h}"))
                t0 = DEC_T * h
                qn = B1[:, t0 * H:t0 * H + 64]
                qr = T1[0:ROPE, t0 * H:t0 * H + 64]
                for n in range(2):
                    mm(PA[0:64, 512 * n:512 * n + 512], qn, kcT[:, 512 * n:512 * n + 512], start=True, stop=False)
                    mm(PA[0:64, 512 * n:512 * n + 512], qr, krcT[0:ROPE, 512 * n:512 * n + 512], start=False, stop=True)
                mm(PA[0:64, 1024:1152], qn, ckvT[:, SEQ:NKEY], start=True, stop=False)
                mm(PA[0:64, 1024:1152], qr, krT[:, SEQ:NKEY], start=False, stop=True).then_inc(pe_done, c.count(f"s S {h}"))
                e.wait_ge(dve_done, c.at("dve", f"s p {h}"))
                for k in range(NKC):
                    m = e.transpose(PB[:, P * k:P * k + 64], PP[0:64, P * k:P * k + P], ident[0:64, 0:64])
                m.then_inc(pe_done, c.count(f"s pT {h}"))
                e.wait_ge(act_done, c.at("act", f"s pT0 {h}"))
                e.wait_ge(dve_done, c.at("dve", f"s pT1 {h}"))
                for k in range(NKC):
                    m = mm(PB[:, 0:64], rows[:, P * k:P * k + P] if k < 8 else ckvR[:, SEQ:NKEY],
                           scr[:, P * k:P * k + 64], start=k == 0, stop=k == NKC - 1)
                m.then_inc(pe_done, c.count(f"s keys used {h}"))
                if h == DEC_B - 1:
                    e.wait_ge(act_done, c.at("act", f"s lat {h}"))
                    for k in range(H):
                        m = mm(PA[0:64, VD * k:VD * k + VD], latS[:, 64 * k:64 * k + 64], w_uv[:, VD * k:VD * k + VD],
                               start=True, stop=True)
                    m.then_inc(pe_done, c.count("s mla"))

            def att(st, T, h):
                if st == "first":
                    return att_sample(h)
                if h == 0:
                    e.wait_ge(act_done, c.at("act", "qlat"))
                    e.wait_ge(act_done, c.at("act", "qrT"))
                    e.wait_ge(S["const"], c.at("const", "all"))
                else:
                    e.wait_ge(act_done, c.at("act", f"mla{h - 1}"))
                for n, (lo, hi) in enumerate(((0, 512), (512, 1024), (1024, 1152))):
                    mm(PA[:, lo:hi], B1[:, P * h:P * h + P], ckvT[:, lo:hi], start=True, stop=False)
                    m = mm(PA[:, lo:hi], T1[0:ROPE, P * h:P * h + P], krT[:, lo:hi], start=False, stop=True)
                m.then_inc(pe_done, c.count(f"S{h}"))
                e.wait_ge(act_done, c.at("act", f"p{h}"))
                transposes(lambda k: PP[:, P * k:P * k + P], NKC, lambda k: PB[:, P * k:P * k + P]).then_inc(pe_done, c.count(f"pT{h}"))
                e.wait_ge(act_done, c.at("act", f"pT0 {h}"))
                e.wait_ge(dve_done, c.at("dve", f"pT1 {h}"))
                for k in range(NKC):
                    m = mm(PA[:, 0:P], ckvR[:, P * k:P * k + P], scr[:, P * k:P * k + P], start=k == 0,
                           stop=k == NKC - 1)
                m.then_inc(pe_done, c.count(f"lat{h}"))
                e.wait_ge(act_done, c.at("act", f"lat{h}"))
                mm(PA[:, 512:512 + VD], latT[:], w_uv[:, VD * h:VD * h + VD], start=True, stop=True).then_inc(pe_done, c.count(f"mla{h}"))

            def out(st, T):
                if st == "first":
                    e.wait_ge(act_done, c.at("act", "s mla"))
                else:
                    e.wait_ge(act_done, c.at("act", f"mla{H - 1}"))
                transposes(lambda k: cat[:, P * k:P * k + P], NCH, lambda k: PB[:, P * k:P * k + P]).then_inc(pe_done, c.count("catT"))
                e.wait_ge(act_done, c.at("act", "catT0"))
                e.wait_ge(dve_done, c.at("dve", "catT1"))
                for k in range(NCH):
                    e.wait_ge(S[f"w{k % 2}"], c.at(f"w{k % 2}", f"o{k}"))
                    for n in range(2):
                        m = mm(PA[:, 512 * n:512 * n + 512], T1[:, P * k:P * k + P], wring[:, k % 2, 512 * n:512 * n + 512],
                               start=k == 0, stop=k == NCH - 1)
                    m.then_inc(pe_done, c.count(f"used o{k}"))

            def gain_rows(row, dst):
                for n in range(2):
                    m = mm(dst[:, 512 * n:512 * n + 512], ones[row:row + 1, :], gains[row:row + 1, 512 * n:512 * n + 512],
                           start=True, stop=True)
                return m

            def norm2(st, T):
                if st == "first":
                    e.wait_ge(S["const"], c.at("const", "all"))
                    e.wait_ge(pool_done, c.at("pool", "cleared"))
                gain_rows(0, PB).then_inc(pe_done, c.count("gffn"))
                e.wait_ge(dve_done, c.at("dve", "h"))
                transposes(lambda k: ha[:, P * k:P * k + P], NCH, lambda k: PA[:, P * k:P * k + P]).then_inc(pe_done, c.count("hT"))

            def query(st, T):
                e.wait_ge(act_done, c.at("act", "hT0"))
                e.wait_ge(dve_done, c.at("dve", "hT1"))
                for k in range(NCH):
                    e.wait_ge(S[f"w{k % 2}"], c.at(f"w{k % 2}", f"q{k}"))
                    for h in range(H):
                        m = mm(PB[:, P * h:P * h + P], wring[:, k % 2, P * h:P * h + P], T1[:, P * k:P * k + P],
                               start=k == 0 and h % 4 == 0, stop=k == NCH - 1, skip_group_check=True)
                    m.then_inc(pe_done, c.count(f"used q{k}"))
                e.wait_ge(act_done, c.at("act", "qT"))
                for h in range(H):
                    dst = PA if h < 4 else PB
                    for p in range(2):
                        o = P * (4 * p + h % 4)
                        m = mm(dst[:, o:o + P], scr[64 * p:64 * p + 64, P * h:P * h + P],
                               keysT[64 * p:64 * p + 64, h, :], start=True, stop=True)
                    if h % 4 == 3:
                        m.then_inc(pe_done, c.count(f"sc{h // 4}"))

            def peer(st, T, g):
                n = nslots(st)
                for j in range(GRP):
                    s = (g - 1) * GRP + j
                    if s < 0:
                        continue
                    e.wait_ge(S[f"gv{s % RING}"], c.at(f"gv{s % RING}", f"v{s}"))
                    e.wait_ge(dve_done, c.at("dve", f"d{s}"))
                    for q in range(2):
                        m = mm(Y[:, 512 * q:512 * q + 512], diag[:, s % RING, :], V[:, s % RING, 512 * q:512 * q + 512],
                               start=s == 0, stop=s == n - 1, skip_group_check=True)
                    m.then_inc(pe_done, c.count(f"v{s}"))

            def tail(st, T):
                if st == "first":
                    e.wait_ge(act_done, c.at("act", "sc1"))
                    return
                e.wait_ge(act_done, c.at("act", "y sq"))
                gain_rows(32, Y).then_inc(pe_done, c.count("gfin"))

            run(c, dict(norm1=norm1, proj=projection, kv=kv, ret1=ret1, ret2=ret2, q1=q1, att=att, out=out,
                        norm2=norm2, query=query), peer, tail, e)

        @block.scalar
        def _(e):
            c = Counter(e, "act")
            act = e.activation

            def by_half(x):
                return x.rearrange("p (q s t) -> p s q t", q=4, s=2)

            def root(dst, ss, n, name):
                e.wait_ge(act_done, c.here())
                act(dst, ss, ACT.Sqrt, bias=epsc[:], scale=1.0 / n).then_inc(act_done, c.count(name))

            def norm1(st, T):
                if st == "first":
                    e.wait_ge(S["ld_id"], c.at("ld_id", "gq"))
                e.wait_ge(S["x_in"], c.at("x_in", "x"))
                act(scr[:, 0:D], xa[:], ACT.Square, accum_out=small[:, 0:1]).then_inc(act_done, c.count())
                root(small[:, 1:2], small[:, 0:1], D, "x sq")
                e.wait_ge(dve_done, c.at("dve", "x rstd"))
                e.wait_ge(act_done, c.here())
                act(scr[:, 0:D], xa[:], ACT.Copy, scale=small[:, 1:2]).then_inc(act_done, c.count("xn"))
                e.wait_ge(pe_done, c.at("pe", "xT"))
                for k in range(4):
                    act(T1[:, P * k:P * k + P], PB[:, P * k:P * k + P], ACT.Copy, scale=gcol[:, k:k + 1]).then_inc(act_done, c.count("xT0" if k == 3 else None))

            def projection(st, T):
                for n in range(5):
                    lo, hi = 512 * n, min(512 * n + 512, IN_W)
                    e.wait_ge(pe_done, c.at("pe", f"proj{n}"))
                    act(proj[:, lo:hi], PA[:, 512 * (n % 3):512 * (n % 3) + hi - lo], ACT.Copy).then_inc(act_done, c.count(f"proj{n}"))

            def kv(st, T):
                e.wait_ge(act_done, c.here())
                act(scr[:, 0:Q_LORA], proj[:, 0:Q_LORA], ACT.Square, accum_out=small[:, 2:3]).then_inc(act_done, c.count())
                act(scr[:, C_KV:C_KV + KV], proj[:, C_KV:C_KV + KV], ACT.Square, accum_out=small[:, 3:4]).then_inc(act_done, c.count())
                root(small[:, 4:5], small[:, 2:3], Q_LORA, None)
                root(small[:, 5:6], small[:, 3:4], KV, "kv sq")
                e.wait_ge(dve_done, c.at("dve", "kv rstd"))
                act(B1[:, 0:Q_LORA], proj[:, 0:Q_LORA], ACT.Copy, scale=small[:, 4:5]).then_inc(act_done, c.count("cqn"))
                at = SEQ if st == "first" else (T - 1) * P
                e.wait_ge(dve_done, c.at("dve", "krope"))
                act(ckvR[:, bass.ds(at, P)], ckvS[:], ACT.Copy).then_inc(act_done, c.count())
                e.wait_ge(pe_done, c.at("pe", "kvT"))
                act(ckvT[:, bass.ds(at, P)], PB[:, 0:P], ACT.Copy).then_inc(act_done, c.count())
                act(krT[:, bass.ds(at, P)], PB[0:ROPE, P:2 * P], ACT.Copy).then_inc(act_done, c.count())
                for k in range(2):
                    act(T1[:, P * k:P * k + P], PB[:, P * (2 + k):P * (3 + k)], ACT.Copy, scale=gq[:, k:k + 1]).then_inc(act_done, c.count("cqT" if k else None))

            def ret1(st, T):
                e.wait_ge(pe_done, c.at("pe", "rT"))
                act(B1[:], PB[:, 512:1536], ACT.Copy).then_inc(act_done, c.count("rT"))
                if st == "first":
                    e.wait_ge(pe_done, c.at("pe", "crossT"))
                    act(by_half(scr[0:64, 0:512]),
                              PB[0:64, 512:1536].rearrange("p (s x) -> p s x", s=2)[:, :, 0:256]
                              .rearrange("p s (q t) -> p s q t", q=4), ACT.Copy).then_inc(act_done, c.count("crossT"))
                e.wait_ge(dve_done, c.at("dve", "o"))
                act(PP[:, 0:512], scr[:, 0:512], ACT.Square).then_inc(act_done, c.count("o sq"))
                act(PP[:, 512:1024], proj[:, C_RG:C_RG + 512], ACT.Exp, scale=-1.0).then_inc(act_done, c.count("exp rg"))

            def ret2(st, T):
                e.wait_ge(dve_done, c.at("dve", "hn ss"))
                root(small[:, 8:16], small[:, 8:16], 64, "hn")

            def q1(st, T):
                e.wait_ge(pe_done, c.at("pe", "q"))
                for n in range(2):
                    src = PA[:, 512 * n:512 * n + 384].rearrange("p (h d) -> p h d", d=96)
                    act(scr[:, 256 * n:256 * n + 256].rearrange("p (h d) -> p h d", d=64), src[:, :, 0:64],
                              ACT.Copy).then_inc(act_done, c.count())
                    act(scr[:, 512 + 128 * n:640 + 128 * n].rearrange("p (h d) -> p h d", d=32),
                              src[:, :, 64:96], ACT.Copy).then_inc(act_done, c.count("q rope in" if n else None))
                e.wait_ge(pe_done, c.at("pe", "qnT"))
                act(PP[:, 0:512], PB[:, 0:512], ACT.Copy).then_inc(act_done, c.count("qnT"))
                e.wait_ge(pe_done, c.at("pe", "qrT"))
                if st == "first":
                    act(T1[0:ROPE, :].rearrange("p (t h) -> p h t", h=H),
                              PB[0:ROPE, 512:1536].rearrange("p (h t) -> p h t", h=H), ACT.Copy).then_inc(act_done, c.count("qrT"))
                else:
                    act(T1[0:ROPE, :], PB[0:ROPE, 512:1536], ACT.Copy).then_inc(act_done, c.count("qrT"))
                e.wait_ge(pe_done, c.at("pe", "qlat"))
                dst = B1[:].rearrange("p (t q s) -> p s q t" if st == "first" else "p (q s t) -> p s q t", q=4, s=2)
                act(dst, PA[:, 0:1024].rearrange("p (s q t) -> p s q t", s=2, q=4), ACT.Copy).then_inc(act_done, c.count("qlat"))

            def att_sample(h):
                e.wait_ge(pe_done, c.at("pe", f"s kT {h}"))
                act(kcT, PB[:, 0:1024], ACT.Copy).then_inc(act_done, c.count(f"s kT {h}"))
                e.wait_ge(dve_done, c.at("dve", f"s nb {h}"))
                act(PP[0:64, :], PP[0:64, :], ACT.Exp, bias=small[0:64, 21:22], scale=SCALE,
                          accum_out=small[0:64, 22:23]).then_inc(act_done, c.count(f"s p {h}"))
                e.wait_ge(pe_done, c.at("pe", f"s pT {h}"))
                act(scr[:, 0:1024].rearrange("p (k r) -> p k r", r=P)[:, :, 0:64],
                          PB[:, 0:1024].rearrange("p (k r) -> p k r", r=P)[:, :, 0:64], ACT.Copy).then_inc(act_done, c.count(f"s pT0 {h}"))
                e.wait_ge(pe_done, c.at("pe", f"s keys used {h}"))
                act(latS.rearrange("p (h t) -> p h t", h=H)[:, :, DEC_T * h:DEC_T * h + DEC_T],
                          PB[:, 0:64].rearrange("p (t h) -> p h t", h=H), ACT.Copy).then_inc(act_done, c.count(f"s lat {h}"))
                if h == DEC_B - 1:
                    e.wait_ge(pe_done, c.at("pe", "s mla"))
                    act(cat[0:64, 0:512], PA[0:64, 0:512], ACT.Copy).then_inc(act_done, c.count("s mla"))

            def att(st, T, h):
                if st == "first":
                    return att_sample(h)
                e.wait_ge(dve_done, c.at("dve", f"nb{h}"))
                act(PP[:], PP[:], ACT.Exp, bias=small[:, 21:22], scale=SCALE, accum_out=small[:, 22:23]).then_inc(act_done, c.count(f"p{h}"))
                e.wait_ge(pe_done, c.at("pe", f"pT{h}"))
                act(scr[:, 0:1024], PB[:, 0:1024], ACT.Copy).then_inc(act_done, c.count(f"pT0 {h}"))
                e.wait_ge(pe_done, c.at("pe", f"lat{h}"))
                act(latT[:], PA[:, 0:P], ACT.Copy).then_inc(act_done, c.count(f"lat{h}"))
                e.wait_ge(dve_done, c.at("dve", f"rl{h}"))
                e.wait_ge(pe_done, c.at("pe", f"mla{h}"))
                act(cat[:, VD * h:VD * h + VD], PA[:, 512:512 + VD], ACT.Copy, scale=small[:, 23:24]).then_inc(act_done, c.count(f"mla{h}"))

            def out(st, T):
                e.wait_ge(pe_done, c.at("pe", "catT"))
                act(T1[:, 0:512], PB[:, 0:512], ACT.Copy).then_inc(act_done, c.count("catT0"))

            def norm2(st, T):
                e.wait_ge(dve_done, c.at("dve", "residual"))
                if st == "first":
                    e.wait_ge(S["dup"], c.at("dup", "dup"))
                act(scr[:, 0:D], xa[:], ACT.Square, accum_out=small[:, 24:25]).then_inc(act_done, c.count())
                root(small[:, 25:26], small[:, 24:25], D, "x2 sq")
                e.wait_ge(pe_done, c.at("pe", "hT"))
                act(T1[:, 0:512], PA[:, 0:512], ACT.Copy).then_inc(act_done, c.count("hT0"))

            def query(st, T):
                e.wait_ge(pe_done, c.at("pe", f"used q{NCH - 1}"))
                act(scr[:, 0:D], PB[:, 0:D], ACT.Copy).then_inc(act_done, c.count("qT"))
                e.wait_ge(pe_done, c.at("pe", "sc0"))
                act(proj[:, 0:1024], PA[:, 0:1024], ACT.Copy).then_inc(act_done, c.count("sc0"))
                e.wait_ge(pe_done, c.at("pe", "sc1"))
                act(proj[:, 1024:2048], PB[:, 0:1024], ACT.Copy).then_inc(act_done, c.count("sc1"))

            def top3(st, T):
                e.wait_ge(dve_done, c.at("dve", "best - max"))
                act(T1[:, 256:384], T1[:, 256:384], ACT.Exp).then_inc(act_done, c.count("gate exp"))

            def peer(st, T, g):
                if g * GRP >= nslots(st):
                    return
                e.wait_ge(dve_done, c.at("dve", f"u{g * GRP + GRP - 1}"))
                if g >= 2:
                    e.wait_ge(dve_done, c.at("dve", f"d{(g - 1) * GRP - 1}"))
                act(acts[:, g % 2, :], dots[:, g % 2, :], ACT.Gelu).then_inc(act_done, c.count(f"gelu{g}"))

            def tail(st, T):
                if st != "first":
                    e.wait_ge(dve_done, c.at("dve", "y sum"))
                    act(Y, xr[:], ACT.Square, accum_out=peerv[:, 0:1]).then_inc(act_done, c.count())
                    root(peerv[:, 1:2], peerv[:, 0:1], D, "y sq")
                if st != "last":
                    e.wait_ge(dve_done, c.at("dve", "handed"))
                    act(hr[:], ha[:], ACT.Copy).then_inc(act_done, c.count())
                    if st != "first":
                        e.wait_ge(S["y_out"], c.at("y_out", "y"))
                    act(xr[:], xa[:], ACT.Copy).then_inc(act_done, c.count("handed"))

            run(c, dict(norm1=norm1, proj=projection, kv=kv, ret1=ret1, ret2=ret2, q1=q1, att=att, out=out,
                        norm2=norm2, query=query, top3=top3), peer, tail, e)

        @block.vector
        def _(e):
            c = Counter(e, "dve")
            tt, ts, stt, red = e.tensor_tensor, e.tensor_scalar, e.scalar_tensor_tensor, e.tensor_reduce

            def invert(x, name=None):
                e.reciprocal(x, x).then_inc(dve_done, c.count(name))

            def settle():
                e.wait_ge(dve_done, c.here())
                e.sem_inc(S["tick_dve"], 1)

            def norm1(st, T):
                if st == "first":
                    e.wait_ge(pool_done, c.at("pool", "iota p"))
                    e.wait_ge(S["pg"], c.at("pg", "pages"))
                    e.tensor_copy(small[:, 91:92], small[:, 90:91].bitcast(I32)).then_inc(dve_done, c.count())
                    pf = ha[:, 0:64]
                    e.wait_ge(pool_done, c.at("pool", "cleared"))
                    e.tensor_copy(PP[:, 0:64], idx_r[:, 64:128].bitcast(I32)).then_inc(dve_done, c.count())
                    e.wait_ge(dve_done, c.here())
                    ts(PP[:, 0:64], PP[:, 0:64], float(P), small[:, 91:92], ALU.mult, ALU.add).then_inc(dve_done, c.count())
                    e.wait_ge(dve_done, c.here())
                    e.tensor_copy(idx_r[:, 0:64], PP[:, 0:64]).then_inc(dve_done, c.count("page rows"))
                    e.wait_ge(S["ld_id"], c.at("ld_id", "gq"))
                e.wait_ge(act_done, c.at("act", "x sq"))
                invert(small[:, 1:2], "x rstd")
                e.wait_ge(pe_done, c.at("pe", "xT"))
                for k in range(4, 8):
                    ts(T1[:, P * k:P * k + P], PB[:, P * k:P * k + P], gcol[:, k:k + 1], None, ALU.mult).then_inc(dve_done, c.count("xT1" if k == 7 else None))

            def rotate(x, n, half, cos, sin, tmpa, tmpb, name):
                xv = x.rearrange("p (n s f) -> p n s f", n=n, s=2)
                a = tmpa.rearrange("p (n s f) -> p n s f", n=n, s=2)
                b = tmpb.rearrange("p (n s f) -> p n s f", n=n, s=2)
                cb = cos.unsqueeze(1).to_broadcast([P, n, half])
                sbc = sin.unsqueeze(1).to_broadcast([P, n, half])
                for s in range(2):
                    tt(a[:, :, s, :], xv[:, :, s, :], cb, ALU.mult).then_inc(dve_done, c.count())
                    tt(b[:, :, s, :], xv[:, :, 1 - s, :], sbc, ALU.mult).then_inc(dve_done, c.count())
                e.wait_ge(dve_done, c.here())
                tt(xv[:, :, 0, :], a[:, :, 0, :], b[:, :, 0, :], ALU.subtract).then_inc(dve_done, c.count())
                tt(xv[:, :, 1, :], a[:, :, 1, :], b[:, :, 1, :], ALU.add).then_inc(dve_done, c.count(name))

            cos32, sin32 = trig[:, 0:32], trig[:, 32:64]
            cos16, sin16 = trig2[:, 0, :, 0], trig2[:, 1, :, 0]

            def kv(st, T):
                e.wait_ge(S["const"], c.at("const", "all"))
                e.wait_ge(act_done, c.at("act", "kv sq"))
                invert(small[:, 4:6], "kv rstd")
                e.tensor_copy(krS[:], proj[:, C_KR:C_KR + ROPE]).then_inc(dve_done, c.count())
                e.wait_ge(dve_done, c.here())
                stt(ckvS[:], proj[:, C_KV:C_KV + KV], small[:, 5:6], gkv[:], ALU.mult, ALU.mult).then_inc(dve_done, c.count())
                rotate(krS[:], 1, 16, cos16, sin16, PP[:, 0:32], PP[:, 32:64], "krope")
                e.wait_ge(dve_done, c.here())
                rotate(proj[:, C_RQ:C_RV], 16, 32, cos32, sin32, scr[:, 0:1024], PP[:, 0:1024], "rope")

            def by_half(x):
                return x.rearrange("p (q s e) -> p s q e", q=4, s=2)

            hb = lambda x: x.unsqueeze(2).to_broadcast([x.shape[0], H, 64])
            hv = lambda x: x.rearrange("p (h d) -> p h d", h=H)

            def ret1(st, T):
                e.wait_ge(dve_done, c.here())
                tt(hv(scr[:, 512:1024]), hv(proj[:, C_RK:C_RK + 512]), hb(kdecc), ALU.mult).then_inc(dve_done, c.count("kd0" if st != "first" else None))
                e.wait_ge(pe_done, c.at("pe", "inner"))
                tt(PP[:, 0:1024].rearrange("p (h i) -> p h i", h=H), PA[:, 0:1024].rearrange("p (h i) -> p h i", h=H),
                         dmat[:], ALU.mult).then_inc(dve_done, c.count("innerT"))
                e.wait_ge(pe_done, c.at("pe", "cross"))
                n = 64 if st == "first" else P
                for a in range(2):
                    src = PB[0:n, 512 + 512 * a:768 + 512 * a].rearrange("p (q e) -> p q e", q=4)
                    f = crossc[0:n, :].rearrange("p (q s) -> p s q", s=2)[:, a, :].unsqueeze(2).to_broadcast([n, 4, 64])
                    tt(by_half(scr[0:n, 0:512])[:, a, :, :], src, f, ALU.mult).then_inc(dve_done, c.count())
                e.wait_ge(pe_done, c.at("pe", "o1"))
                e.wait_ge(dve_done, c.here())
                if st == "first":
                    e.tensor_copy(scr[64:P, 0:512], PB[64:P, 0:512]).then_inc(dve_done, c.count())
                tt(scr[0:n, 0:512], PB[0:n, 0:512], scr[0:n, 0:512], ALU.add).then_inc(dve_done, c.count("o"))

            def ret2(st, T):
                gb = lambda x, m: x.unsqueeze(1).unsqueeze(3).to_broadcast([P, m, 4, 64])
                if st == "first":
                    e.wait_ge(dve_done, c.here())
                    for b in range(DEC_B + 1):
                        if b < DEC_B:
                            tt(sst[:, b, :, :], sst[:, b, :, :], gchunk.unsqueeze(2).to_broadcast([P, 4, 64]),
                                     ALU.mult).then_inc(dve_done, c.count())
                        if b >= 2:
                            e.wait_ge(pe_done, c.at("pe", f"su{b - 2}"))
                        ts(kdb[:, 512 * (b % 2):512 * (b % 2) + 512], scr[:, 512:1024], onehot[:, b:b + 1], None,
                                 ALU.mult).then_inc(dve_done, c.count(f"kd{b}"))
                        if b >= 1:
                            add_states(b - 1)
                    add_states(DEC_B)
                else:
                    e.wait_ge(pe_done, c.at("pe", "su0"))
                    tt(state[:], state[:], gchunk.unsqueeze(2).to_broadcast([P, 4, 64]), ALU.mult).then_inc(dve_done, c.count())
                    e.wait_ge(dve_done, c.here())
                    for a in range(2):
                        r = slice(64 * a, 64 * a + 64)
                        up = PA[r, 0:512].rearrange("p (q e) -> p q e", q=4)[:, :, 64 * a:64 * a + 64]
                        tt(state[r, :, :], up, state[r, :, :], ALU.add).then_inc(dve_done, c.count())
                e.wait_ge(act_done, c.at("act", "exp rg"))
                e.wait_ge(dve_done, c.here())
                red(small[:, 8:16], hv(PP[:, 0:512]), AX, ALU.add).then_inc(dve_done, c.count("hn ss"))
                ts(PP[:, 512:1024], PP[:, 512:1024], 1.0, None, ALU.add).then_inc(dve_done, c.count())
                e.wait_ge(dve_done, c.here())
                e.reciprocal(PP[:, 512:1024], PP[:, 512:1024]).then_inc(dve_done, c.count())
                e.wait_ge(act_done, c.at("act", "hn"))
                invert(small[:, 8:16])
                e.wait_ge(dve_done, c.here())
                tt(PP[:, 512:1024], PP[:, 512:1024], proj[:, C_RG:C_RG + 512], ALU.mult).then_inc(dve_done, c.count())
                tt(hv(scr[:, 0:512]), hv(scr[:, 0:512]), hb(small[:, 8:16]), ALU.mult).then_inc(dve_done, c.count())
                e.wait_ge(dve_done, c.here())
                if st == "first":
                    e.wait_ge(pool_done, c.at("pool", "cleared"))
                tt(cat[:, 512:1024], scr[:, 0:512], PP[:, 512:1024], ALU.mult).then_inc(dve_done, c.count("ret"))

            def add_states(b):
                e.wait_ge(pe_done, c.at("pe", f"su{b}"))
                e.wait_ge(dve_done, c.here())
                for a in range(2):
                    r = slice(64 * a, 64 * a + 64)
                    up = PA[r, 512 * (b % 2):512 * (b % 2) + 512].rearrange("p (q e) -> p q e", q=4)[:, :, 64 * a:64 * a + 64]
                    if b < DEC_B:
                        tt(sst[r, b, :, :], up, sst[r, b, :, :], ALU.add).then_inc(dve_done, c.count(None if a == 0 else f"sn{b}"))
                    else:
                        e.tensor_copy(state[r, :, :], up).then_inc(dve_done, c.count("states" if a else None))

            def q1(st, T):
                e.wait_ge(act_done, c.at("act", "q rope in"))
                e.wait_ge(dve_done, c.here())
                rotate(scr[:, 512:768], H, 16, cos16, sin16, PP[:, 512:768], PP[:, 768:1024], "q rope")

            def att_sample(h):
                e.wait_ge(pe_done, c.at("pe", f"s krT {h}"))
                e.tensor_copy(krcT[0:ROPE, :], PA[0:ROPE, 0:1024]).then_inc(dve_done, c.count(f"s krT {h}"))
                e.wait_ge(pe_done, c.at("pe", f"s S {h}"))
                e.tensor_copy(PP[0:64, 0:1024], PA[0:64, 0:1024]).then_inc(dve_done, c.count())
                lo = 120 - DEC_T * h
                tt(PP[0:64, 1024:1152], PA[0:64, 1024:1152], newm[:, lo:lo + P], ALU.add).then_inc(dve_done, c.count())
                e.wait_ge(dve_done, c.here())
                red(small[0:64, 20:21], PP[0:64, :], AX, ALU.max).then_inc(dve_done, c.count())
                e.wait_ge(dve_done, c.here())
                ts(small[0:64, 21:22], small[0:64, 20:21], -SCALE, None, ALU.mult).then_inc(dve_done, c.count(f"s nb {h}"))
                e.wait_ge(act_done, c.at("act", f"s p {h}"))
                e.reciprocal(small[0:64, 23:24], small[0:64, 22:23]).then_inc(dve_done, c.count())
                e.wait_ge(dve_done, c.here())
                ts(PP[0:64, :], PP[0:64, :], small[0:64, 23:24], None, ALU.mult).then_inc(dve_done, c.count(f"s p {h}"))
                e.wait_ge(pe_done, c.at("pe", f"s pT {h}"))
                e.tensor_copy(scr[:, 1024:1088], PB[:, 1024:1088]).then_inc(dve_done, c.count(f"s pT1 {h}"))

            def att(st, T, h):
                if st == "first":
                    return att_sample(h)
                e.wait_ge(pe_done, c.at("pe", f"S{h}"))
                e.sem_inc(S["tick_dve"], 1)
                e.tensor_tensor_reduce(PP[:], PA[:, 0:NKEY], mask, 1.0, NEG, ALU.add, ALU.max, small[:, 20:21]).then_inc(dve_done, c.count())
                e.wait_ge(dve_done, c.here())
                ts(small[:, 21:22], small[:, 20:21], -SCALE, None, ALU.mult).then_inc(dve_done, c.count(f"nb{h}"))
                e.wait_ge(act_done, c.at("act", f"p{h}"))
                e.reciprocal(small[:, 23:24], small[:, 22:23]).then_inc(dve_done, c.count(f"rl{h}"))
                e.wait_ge(pe_done, c.at("pe", f"pT{h}"))
                e.tensor_copy(scr[:, 1024:1152], PB[:, 1024:1152]).then_inc(dve_done, c.count(f"pT1 {h}"))

            def out(st, T):
                e.wait_ge(pe_done, c.at("pe", "catT"))
                e.tensor_copy(T1[:, 512:1024], PB[:, 512:1024]).then_inc(dve_done, c.count("catT1"))
                e.wait_ge(pe_done, c.at("pe", f"used o{NCH - 1}"))
                tt(xa[:], PA[:, 0:D], xa[:], ALU.add).then_inc(dve_done, c.count("residual"))

            def norm2(st, T):
                e.wait_ge(act_done, c.at("act", "x2 sq"))
                invert(small[:, 25:26])
                e.wait_ge(pe_done, c.at("pe", "gffn"))
                e.wait_ge(dve_done, c.here())
                stt(ha[:], xa[:], small[:, 25:26], PB[:, 0:D], ALU.mult, ALU.mult).then_inc(dve_done, c.count("h"))
                e.wait_ge(pe_done, c.at("pe", "hT"))
                e.tensor_copy(T1[:, 512:1024], PA[:, 512:1024]).then_inc(dve_done, c.count("hT1"))

            NL = 2 * H
            val = B1[:, 0:256].rearrange("p (l k) -> p l k", l=NL)
            ival = B1[:, 256:512].bitcast(U32).rearrange("p (l k) -> p l k", l=NL)
            fval = B1[:, 512:768].rearrange("p (h s k) -> p h s k", h=H, s=2)
            valp = B1[:, 0:256].rearrange("p (h s k) -> p h s k", h=H, s=2)
            cnd = PP[:, 0:H * NPAIR].rearrange("p (h c) -> p h c", h=H)
            cnde = PP[:, H * NPAIR:2 * H * NPAIR].rearrange("p (h c) -> p h c", h=H)
            best = PP[:, 800:928].rearrange("p (h k) -> p h k", h=H)
            bpos = PP[:, 928:1056].bitcast(U32).rearrange("p (h k) -> p h k", h=H)
            bposf = T1[:, 0:P].rearrange("p (h k) -> p h k", h=H)
            ef = T1[:, P:2 * P]
            gd = T1[:, 2 * P:3 * P]

            def top16(src, n, width, value, index):
                for half in range(2):
                    lo, hi = 8 * half, 8 * half + 8
                    settle()
                    for l in range(n):
                        e.max(value[:, l, lo:hi], src(l)).then_inc(dve_done, c.count())
                    settle()
                    for l in range(n):
                        e.max_index(index[:, l, lo:hi], value[:, l, lo:hi], src(l)).then_inc(dve_done, c.count())
                    if half == 0:
                        settle()
                        for l in range(n):
                            e.match_replace(src(l), value[:, l, lo:hi], src(l), NEG).then_inc(dve_done, c.count())

            def score_at(l):
                h, p = l // 2, l % 2
                return 1024 * (h // 4) + 512 * p + P * (h % 4)

            def top1(st, T):
                e.wait_ge(act_done, c.at("act", "sc1"))
                top16(lambda l: proj[:, score_at(l):score_at(l) + P], NL, P, val, ival)

            def top2(st, T):
                e.wait_ge(dve_done, c.here())
                e.tensor_copy(B1[:, 512:768], B1[:, 256:512].bitcast(U32)).then_inc(dve_done, c.count())
                e.wait_ge(dve_done, c.here())
                ts(fval[:, :, 0, :], fval[:, :, 0, :], 128.0, None, ALU.mult).then_inc(dve_done, c.count())
                e.wait_ge(dve_done, c.here())
                for src, dst in ((valp, cnd), (fval, cnde)):
                    at = 0
                    for a in range(8):
                        w = TOPK // (a + 1)
                        tt(dst[:, :, at:at + w], src[:, :, 0, a:a + 1].to_broadcast([P, H, w]),
                                 src[:, :, 1, 0:w], ALU.add).then_inc(dve_done, c.count())
                        at += w
                    tt(dst[:, :, at:at + 8], src[:, :, 0, 8:16], src[:, :, 1, 0:1].to_broadcast([P, H, 8]),
                             ALU.add).then_inc(dve_done, c.count())
                top16(lambda l: cnd[:, l, :], H, NPAIR, best, bpos)

            def top3(st, T):
                e.wait_ge(dve_done, c.here())
                tt(gd.rearrange("p (h k) -> p h k", h=H), best, best[:, :, 0:1].to_broadcast([P, H, TOPK]),
                         ALU.subtract).then_inc(dve_done, c.count("best - max"))
                e.tensor_copy(T1[:, 0:P], PP[:, 928:1056].bitcast(U32)).then_inc(dve_done, c.count())
                eq = proj[:, 0:2 * TOPK * NPAIR].rearrange("p (k c) -> p k c", c=NPAIR)
                for q in range(4):
                    for r in range(2):
                        h = 2 * q + r
                        v = eq[:, TOPK * r:TOPK * r + TOPK, :]
                        e.wait_ge(dve_done, c.here())
                        tt(v, bposf[:, h, :].unsqueeze(2).to_broadcast([P, TOPK, NPAIR]),
                                 iota[:].unsqueeze(1).to_broadcast([P, TOPK, NPAIR]), ALU.is_equal).then_inc(dve_done, c.count())
                        e.wait_ge(dve_done, c.here())
                        tt(v, v, cnde[:, h, :].unsqueeze(1).to_broadcast([P, TOPK, NPAIR]), ALU.mult).then_inc(dve_done, c.count())
                    e.wait_ge(dve_done, c.here())
                    red(ef[:, 32 * q:32 * q + 32], eq, AX, ALU.add).then_inc(dve_done, c.count())
                e.wait_ge(dve_done, c.here())
                e.tensor_copy(idx_a[:], ef).then_inc(dve_done, c.count())
                e.wait_ge(act_done, c.at("act", "gate exp"))
                gv = gd.rearrange("p (h k) -> p h k", h=H)
                red(small[:, 30:38], gv, AX, ALU.add).then_inc(dve_done, c.count())
                e.wait_ge(dve_done, c.here())
                e.reciprocal(small[:, 30:38], small[:, 30:38]).then_inc(dve_done, c.count())
                e.wait_ge(dve_done, c.here())
                tt(gate_a[:].rearrange("p (h k) -> p h k", h=H), gv,
                         small[:, 30:38].unsqueeze(2).to_broadcast([P, H, TOPK]), ALU.mult).then_inc(dve_done, c.count())

            def peer(st, T, g):
                n = nslots(st)
                for j in range(GRP):
                    s = g * GRP + j
                    if s < n:
                        if j == 0 and g >= 2:
                            e.wait_ge(act_done, c.at("act", f"gelu{g - 2}"))
                        e.wait_ge(S[f"gu{s % RING}"], c.at(f"gu{s % RING}", f"u{s}"))
                        e.tensor_tensor_reduce(U[:, s % RING, :], U[:, s % RING, :], hr[:], 1.0, 0.0, ALU.mult,
                                                     ALU.add, dots[:, g % 2, j:j + 1]).then_inc(dve_done, c.count(f"u{s}"))
                    s -= GRP
                    if s >= 0:
                        if j == 0:
                            e.wait_ge(act_done, c.at("act", f"gelu{g - 1}"))
                        if s >= RING:
                            e.wait_ge(pe_done, c.at("pe", f"v{s - RING}"))
                        m = (fold if st == "second" else ident)[:]
                        ts(diag[:, s % RING, :], m, acts[:, (g - 1) % 2, j:j + 1], gate_r[:, s:s + 1],
                                 ALU.mult, ALU.mult).then_inc(dve_done, c.count(f"d{s}"))

            def tail(st, T):
                if st != "first":
                    e.wait_ge(pe_done, c.at("pe", f"v{nslots(st) - 1}"))
                    tt(xr[:], Y, xr[:], ALU.add).then_inc(dve_done, c.count("y sum"))
                    e.wait_ge(act_done, c.at("act", "y sq"))
                    invert(peerv[:, 1:2])
                    e.wait_ge(pe_done, c.at("pe", "gfin"))
                    e.wait_ge(dve_done, c.here())
                    stt(xr[:], xr[:], peerv[:, 1:2], Y, ALU.mult, ALU.mult).then_inc(dve_done, c.count("y"))
                if st != "last":
                    e.wait_ge(dve_done, c.here())
                    if st == "first":
                        for src, dst in ((idx_a, idx_r), (gate_a, gate_r)):
                            e.tensor_copy(dst[0:64, 0:64], src[0:64, 0:64]).then_inc(dve_done, c.count())
                            e.tensor_copy(dst[64:P, 0:64], src[64:P, 64:P]).then_inc(dve_done, c.count(None if dst is idx_r else "handed"))
                    else:
                        e.tensor_copy(idx_r[:], idx_a[:]).then_inc(dve_done, c.count())
                        e.tensor_copy(gate_r[:], gate_a[:]).then_inc(dve_done, c.count("handed"))
                e.wait_ge(act_done, c.at("act", "handed")) if st != "last" else None

            run(c, dict(norm1=norm1, kv=kv, ret1=ret1, ret2=ret2, q1=q1, att=att, out=out, norm2=norm2, top1=top1,
                        top2=top2, top3=top3), peer, tail, e)

    return new_counts, new_marks


def _apart(dm):
    return np.ascontiguousarray(dm[:, [0, 2, 4, 6, 1, 3, 5, 7], :])


def shape_constants():
    f = np.float32
    r = np.arange(P)
    pos = np.zeros((NTILE + 1, P))
    pos[0, 0:NSMP] = PAGES * P + np.arange(NSMP) % DEC_T
    pos[0, NSMP:NSMP + N_META] = np.arange(N_META)
    for t in range(1, NTILE + 1):
        pos[t] = N_META + (t - 1) * P + r
    inv = (f(10000.0) ** (-np.arange(32, dtype=f) / f(32))).astype(f)
    ang = (pos.astype(f)[:, :, None] * inv).astype(f)
    trig = np.concatenate([np.cos(ang), np.sin(ang)], axis=2).reshape(-1, 64).astype(f)
    lg = np.log(1.0 - 2.0 ** (-5.0 - np.arange(H)))

    def tables(start, length):
        i = r - start
        rel = r[None, :] - r[:, None]
        ok = (rel >= 0) & (start[None, :] == start[:, None]) & (length[None, :] > 0)
        d = np.exp(lg[:, None, None] * np.maximum(rel, 0)) * ok / 8.0
        dm = d.transpose(1, 0, 2).astype(f)
        cross = np.exp(lg[None, :] * (i[:, None] + 1.0))
        kdec = np.exp(lg[None, :] * (length[:, None] - 1.0 - i[:, None])) / 8.0 * (length[:, None] > 0)
        return dm, cross, kdec

    out = {}
    for n in range(2):
        if n == 0:
            start = np.where(r < NSMP, r // DEC_T * DEC_T, NSMP)
            length = np.where(r < NSMP, DEC_T, np.where(r < NSMP + N_META, N_META, 0))
            chunk = DEC_T
        else:
            start, length, chunk = np.zeros(P, int), np.full(P, P), P
        dm, cross, kdec = tables(start, length)
        one = np.zeros((P, 9))
        for b in range(DEC_B):
            one[DEC_T * b:DEC_T * b + DEC_T, b] = 1
        one[NSMP:NSMP + N_META, DEC_B] = 1
        gch = np.exp(lg[2 * np.arange(4)[None, :] + (r[:, None] >= 64)] * chunk)
        out[f"c_dmat{n}"] = _apart(dm)
        out[f"c_row{n}"] = np.concatenate([one, cross, kdec, gch], axis=1).astype(f)
    mask = np.full((NTILE + 1, P, NKEY), NEG, f)
    mask[:, :, SEQ + NSMP:SEQ + NSMP + N_META] = 0
    for t in range(1, NTILE + 1):
        mask[t, :, 0:SEQ][np.arange(SEQ)[None, :] <= (t - 1) * P + r[:, None]] = 0
    upper = lambda x: (np.ascontiguousarray(x, dtype=f).view(np.uint32) >> 16).astype(np.uint16)
    new = np.full((64, 248), NEG, f)
    for row in range(64):
        new[row, 120:121 + row // H] = 0
    out.update(c_ident=np.eye(P, dtype=f), c_trig=trig,
               c_fold=(r[:, None] % 64 == r[None, :] % 64).astype(f),
               c_iota=np.broadcast_to(np.arange(NPAIR, dtype=f), (P, NPAIR)).copy(),
               c_mask=upper(mask.reshape(-1, NKEY)), c_new=upper(new))
    return out


_INS = ["x_prompt", "x_sample", "cache_ckv", "cache_krope", "state_ret", "page_table", "meta_tokens", "w_in", "w_uq", "g_kv", "w_uv", "w_out", "g_ffn", "w_query", "u_experts", "v_experts", "g_final"]
_OUTS = dict(o_yp=(SEQ, D), o_ys=(NSMP, D), o_ckv_p=(SEQ + N_META, KV), o_kr_p=(SEQ + N_META, ROPE),
             o_ckv_s=(NSMP, KV), o_kr_s=(NSMP, ROPE), o_rp=(H, 64, 64), o_rs=(DEC_B, H, 64, 64))


def kernel(**inputs):
    import numpy as _np
    import concourse.bacc as _bacc
    from concourse import mybir as _mybir
    from concourse.bass_utils import run_bass_kernel_spmd as _run

    arrays = {n: _np.ascontiguousarray(inputs[n]) for n in _INS}
    arrays["t_uk"] = _np.ascontiguousarray(
        _np.asarray(inputs["w_uk"])[0].reshape(KV, 4, 2, NOPE).transpose(2, 3, 1, 0).reshape(P, 4, KV))
    arrays["t_keys"] = _np.ascontiguousarray(
        _np.asarray(inputs["sub_keys"])[0].transpose(1, 3, 0, 2).reshape(P, H, P))
    arrays["t_gcol"] = _np.ascontiguousarray(_np.concatenate(
        [_np.asarray(inputs["g_mix"]).reshape(NCH, P), _np.asarray(inputs["g_q"]).reshape(2, P)]).T)
    arrays.update(shape_constants())
    counts, marks = {}, {}
    for emission in range(2):
        nc = _bacc.Bacc("TRN2", target_bir_lowering=False, num_devices=1)
        args = {n: nc.dram_tensor(f"in_{n}", a.shape, _mybir.dt.from_np(a.dtype), kind="ExternalInput").ap()
                for n, a in arrays.items()}
        args.update({n: nc.dram_tensor(n, s, _mybir.dt.float32, kind="ExternalOutput").ap() for n, s in _OUTS.items()})
        counts, marks = build(nc, args, counts, marks)
    got = _run(nc, [{f"in_{n}": a for n, a in arrays.items()}], core_ids=[0]).results[0]
    return (got["o_yp"].reshape(1, SEQ, D), got["o_ys"].reshape(DEC_B, DEC_T, D),
            got["o_ckv_p"].reshape(1, 1, SEQ + N_META, KV), got["o_kr_p"].reshape(1, 1, SEQ + N_META, ROPE),
            got["o_ckv_s"].reshape(1, DEC_B, DEC_T, KV), got["o_kr_s"].reshape(1, DEC_B, DEC_T, ROPE),
            got["o_rp"].reshape(1, 1, H, 64, 64), got["o_rs"].reshape(1, DEC_B, H, 64, 64))
```

```python
from contextlib import ExitStack

import numpy as np
import concourse.bass as bass
from concourse import mybir

F32 = mybir.dt.float32
BF16 = mybir.dt.bfloat16
U32 = mybir.dt.uint32
U16 = mybir.dt.uint16
I32 = mybir.dt.int32
ACT = mybir.ActivationFunctionType
ALU = mybir.AluOpType
AX = mybir.AxisListType.X

P = 128
D = 1024
NCH = D // P
SEQ = 1024
N_META = 16
NTILE = SEQ // P
DEC_B, DEC_T = 8, 8
NSMP = DEC_B * DEC_T
H = 8
Q_LORA, KV, NOPE, ROPE, VD = 256, 128, 64, 32, 64
IN_W = Q_LORA + KV + ROPE + 4 * H * 64
C_KV, C_KR, C_RQ, C_RK, C_RV, C_RG = 256, 384, 416, 928, 1440, 1952
SCALE = (NOPE + ROPE) ** -0.5
EPS = 1e-6
NKEY = SEQ + P
NKC = NKEY // P
PAGES = 8
TOPK = 16
NEG = -3.0e38
RING = 4
GRP = 8
PAIRS = [(a, b) for a in range(TOPK) for b in range(TOPK) if (a + 1) * (b + 1) <= TOPK]
NPAIR = len(PAIRS)

STRETCHES = ("first", "second", "loop", "last")
LOOP0 = 2


def build(nc, A, counts, marks):
    new_counts, new_marks = {}, {}
    ctx = ExitStack()
    with ctx:
        def sb(name, shape, dt=F32):
            return ctx.enter_context(nc.sbuf_tensor(name, shape, dt))

        def sem(name):
            return ctx.enter_context(nc.semaphore(name))

        w_in = sb("w_in", [P, NCH, IN_W])
        w_uq = sb("w_uq", [P, 2, H * 96])
        ukT = sb("ukT", [P, 4, KV])
        w_uv = sb("w_uv", [P, H * VD])
        keysT = sb("keysT", [P, H, P])
        gains = sb("gains", [33, D])
        gcol = sb("gcol", [P, NCH + 2])
        gkv = sb("gkv", [P, KV])
        ident = sb("ident", [P, P])
        fold = sb("fold", [P, P])
        ones = sb("ones", [33, P])
        dmat = sb("dmat", [P, H, P])
        rowc = sb("rowc", [P, 29])
        trig = sb("trig", [P, 64])
        iota = sb("iota", [P, NPAIR])
        mask16 = sb("mask16", [P, NKEY], U16)
        ckvT = sb("ckvT", [P, NKEY])
        krT = sb("krT", [ROPE, NKEY])
        ckvR = sb("ckvR", [P, NKEY])
        state = sb("state", [P, 4, 64])
        wring = sb("wring", [P, 2, D])
        xa = sb("xa", [P, D])
        ha = sb("ha", [P, D])
        T1 = sb("T1", [P, D])
        B1 = sb("B1", [P, D])
        proj = sb("proj", [P, IN_W])
        PP = sb("PP", [P, NKEY])
        scr = sb("scr", [P, NKEY])
        ckvS = sb("ckvS", [P, KV])
        krS = sb("krS", [P, ROPE])
        small = sb("small", [P, 96])
        latT = sb("latT", [P, P])
        idx_a = sb("idx_a", [P, P], U32)
        gate_a = sb("gate_a", [P, P])
        xr = sb("xr", [P, D])
        hr = sb("hr", [P, D])
        idx_u = sb("idx_u", [P, P], U32)
        idx_v = sb("idx_v", [P, P], U32)
        gate_r = sb("gate_r", [P, P])
        U = sb("U", [P, RING, D])
        V = sb("V", [P, RING, D])
        diag = sb("diag", [P, RING, P])
        dots = sb("dots", [P, 2, GRP])
        acts = sb("acts", [P, 2, GRP])
        peerv = sb("peerv", [P, 4])
        epsc = sb("epsc", [P, 1])
        PS = ctx.enter_context(nc.psum_tensor("PS", [P, 8 * 512], F32))
        Y = PS[:, 0:1024]
        PA = PS[:, 1024:2560]
        PB = PS[:, 2560:4096]

        def apart(h):
            return 4 * (h % 2) + h // 2

        def cross_at(h):
            return 512 + 512 * (h % 2) + 64 * (h // 2)

        gq = gcol[:, NCH:NCH + 2]
        onehot, crossc, kdecc, gchunk = rowc[:, 0:9], rowc[:, 9:17], rowc[:, 17:25], rowc[:, 25:29]
        cat = ha
        cachev = U[:, 0, :]
        kcT = U[:, 1, :]
        krcT = U[:, 2, :]
        krc = U[:, 3, :]
        latS = U[:, 3, 512:1024]
        sst = V[:, 0:2, :].rearrange("p a (b c e) -> p (a b) c e", b=4, c=4)
        mask = mask16[:].bitcast(BF16)
        newm = mask[0:64, 0:248]
        kdb = U[:, 1, :]
        trig2 = trig[:].rearrange("p (s f two) -> p s f two", s=2, two=2)

        names = ["dve", "act", "pe", "pool"] + [f"gu{i}" for i in range(RING)] + [f"gv{i}" for i in range(RING)] + \
            ["w0", "w1", "x_in", "ld_id", "const", "kv_out", "y_out", "ld_w", "st_in", "st_out", "pg"] + \
            [f"win{n}" for n in range(5)] + ["tick_dve", "tick_pool", "tick_sp"] + \
            ["cache0", "cache1", "dup"]
        S = {n: sem({"dve": "dve_done", "act": "act_done", "pe": "pe_done", "pool": "pool_done"}.get(n, n))
             for n in names}

        dve_done, act_done, pe_done, pool_done = S["dve"], S["act"], S["pe"], S["pool"]

        def start(s, st, T):
            c = lambda x: counts.get((s, x), 0)
            if st == "first":
                return 0
            if st == "second":
                return c("first")
            if st == "loop":
                return T * c("loop") + (c("first") + c("second") - LOOP0 * c("loop"))
            return c("first") + c("second") + (NTILE + 1 - LOOP0) * c("loop")

        class Counter:
            def __init__(self, eng, own):
                self.eng, self.own, self.st, self.T = eng, own, "first", 0

            def count(self, name=None, s=None, by=1):
                s = s or self.own
                new_counts[(s, self.st)] = new_counts.get((s, self.st), 0) + by
                if name is not None:
                    assert (s, self.st, name) not in new_marks, (s, self.st, name)
                    new_marks[(s, self.st, name)] = new_counts[(s, self.st)]
                return by

            def at(self, s, name):
                assert not marks or (s, self.st, name) in marks, (s, self.st, name)
                return start(s, self.st, self.T) + marks.get((s, self.st, name), 1)

            def begun(self, s):
                return start(s, self.st, self.T)

            def here(self):
                return start(self.own, self.st, self.T) + new_counts[(self.own, self.st)]

            def meet(self, st, T):
                self.st, self.T = st, T
                if st != "first" and self.own != "pool":
                    for s in ("dve", "act", "pe"):
                        self.eng.wait_ge(S[s], start(s, st, T))
                        if self.own == "sp":
                            self.eng.sem_inc(S["tick_" + self.own], 1)

        MIX = [("norm1", 4), ("proj", 5), ("kv", 3), ("ret1", 6), ("ret2", 3), ("q1", 5)] + \
            [(f"att{h}", 4) for h in range(H)] + \
            [("attend", 4), ("out", 5), ("norm2", 3), ("query", 5), ("top1", 5), ("top2", 3), ("top3", 5)]

        def nslots(st):
            return NSMP if st == "second" else P

        def plan(st):
            turns = nslots(st) + GRP if st != "first" else 0
            parts = sum(k for _, k in MIX)
            out, n = [], 0
            if st == "last":
                return [(None, 0, turns)]
            for m, k in MIX:
                for part in range(k):
                    n += 1
                    out.append((m, part, max(0, (turns - GRP) * n // parts)))
            out.append((None, 0, turns))
            return out

        def run(c, steps, peer, tail, eng):
            def stretch(st, T):
                c.meet(st, T)
                if "begin" in steps:
                    steps["begin"](st, T)
                slot, gen = 0, iter(())
                for m, part, upto in plan(st):
                    if m is not None:
                        if part == 0:
                            for _ in gen:
                                pass
                            key = m[:3] if m.startswith("att") and m != "attend" else m
                            gen = iter(())
                            if key in steps:
                                gen = steps[key](st, T, int(m[3:])) if key == "att" else steps[key](st, T)
                        next(gen, None)
                    else:
                        for _ in gen:
                            pass
                    while slot < upto:
                        if peer is not None:
                            peer(st, T, slot)
                        slot += 1
                tail(st, T)

            stretch("first", 0)
            stretch("second", 1)
            with eng.Fori(LOOP0, NTILE + 1) as T:
                stretch("loop", T)
            stretch("last", NTILE + 1)

        block = ctx.enter_context(nc.Block())

        @block.sync
        def _(e):
            c = Counter(e, "sp")

            def dma(out, in_, s, name):
                e.dma_start(out, in_).then_inc(S[s], c.count(name, s, 16))

            def norm1(st, T):
                yield from ()
                if st == "first":
                    e.wait_ge(pool_done, c.at("pool", "x cleared"))
                    e.sem_inc(S["tick_sp"], 1)
                    dma(xa[0:NSMP, :], A["x_sample"].rearrange("b t d -> (b t) d"), "x_in", "xs")
                    dma(xa[NSMP:NSMP + N_META, :], A["meta_tokens"], "x_in", "x")
                    dma(ident[:], A["c_ident"], "ld_id", "i")
                    dma(gcol[:], A["t_gcol"], "ld_id", "gq")
                    src = A["w_in"].rearrange("o (c p) n -> p (o c) n", p=P)
                    for n in range(5):
                        dma(w_in[:, :, 512 * n:min(512 * n + 512, IN_W)], src[:, :, 512 * n:min(512 * n + 512, IN_W)],
                            f"win{n}", "w")
                    dma(gkv[:], A["g_kv"].rearrange("o k -> (o k)").partition_broadcast(P), "const", "gkv")
                    dma(trig[:], A["c_trig"][0:P, :], "const", "trig")
                    dma(rowc[:], A["c_row0"], "const", "rowc")
                    dma(dmat[:], A["c_dmat0"], "const", "dmat")
                    dma(fold[:], A["c_fold"], "const", "fold")
                    dma(iota[:], A["c_iota"], "const", "iota")
                    dma(mask16[0:64, 0:248], A["c_new"], "const", "newm")
                    dma(gains[0:1, :], A["g_ffn"], "const", "gffn")
                    dma(gains[32:33, :], A["g_final"].rearrange("(o k) -> o k", o=1), "const", "all")
                    st_in = A["state_ret"].rearrange("o b (c a) d e -> (o a) d b c e", a=2)
                    for a in range(2):
                        for b in range(DEC_B):
                            dma(sst[64 * a:64 * a + 64, b, :, :], st_in[a, :, b, :, :], "st_in", f"s{a}{b}")
                    dma(w_uq[:], A["w_uq"].rearrange("o (c p) h d -> p (o c) (h d)", p=P), "ld_w", "w_uq")
                    dma(ukT[:], A["t_uk"], "ld_w", "ukT")
                    dma(w_uv[:], A["w_uv"].rearrange("o c h d -> c (o h d)"), "ld_w", "w_uv")
                    dma(keysT[:], A["t_keys"], "ld_w", "all")
                else:
                    e.wait_ge(act_done, c.at("act", "xr"))
                    e.sem_inc(S["tick_sp"], 1)
                    row = (T - 1) * P
                    dma(xa[:], A["x_prompt"].rearrange("b t d -> (b t) d")[bass.ds(row, P), :], "x_in", "x")
                    dma(trig[:], A["c_trig"][bass.ds(T * P, P), :], "const", "trig")
                    if st == "second":
                        dma(rowc[:], A["c_row1"], "const", "rowc")
                        dma(dmat[:], A["c_dmat1"], "const", "dmat")
                    dma(mask16[:], A["c_mask"][bass.ds(T * P, P), :], "const", "all")

            def kv(st, T):
                yield from ()
                e.wait_ge(dve_done, c.at("dve", "krope"))
                e.sem_inc(S["tick_sp"], 1)
                if st == "first":
                    dma(A["o_ckv_s"], ckvS[0:NSMP, :], "kv_out", "a")
                    dma(A["o_kr_s"], krS[0:NSMP, :], "kv_out", "b")
                    dma(A["o_ckv_p"][0:N_META, :], ckvS[NSMP:NSMP + N_META, :], "kv_out", "c")
                    dma(A["o_kr_p"][0:N_META, :], krS[NSMP:NSMP + N_META, :], "kv_out", "stored")
                else:
                    row = (T - 1) * P + N_META
                    dma(A["o_ckv_p"][bass.ds(row, P), :], ckvS[:], "kv_out", "a")
                    dma(A["o_kr_p"][bass.ds(row, P), :], krS[:], "kv_out", "stored")

            def ret2(st, T):
                yield from ()
                if st == "first":
                    e.wait_ge(dve_done, c.at("dve", "states"))
                    e.sem_inc(S["tick_sp"], 1)
                    out = A["o_rs"].rearrange("b (c a) d e -> a d b c e", a=2)
                    for a in range(2):
                        for b in range(DEC_B):
                            dma(out[a, :, b, :, :], sst[64 * a:64 * a + 64, b, :, :], "st_out", f"o{a}{b}")

            def stream(st, which):
                w = A[which].rearrange("o k n -> (o k) n")
                for k in range(NCH):
                    q = ("o" if which == "w_out" else "q") + str(k)
                    if which == "w_query" or k >= 2:
                        prev = ("o" if (which == "w_out" or k < 2) else "q") + str((k - 2) % NCH)
                        e.wait_ge(pe_done, c.at("pe", "used " + prev))
                        e.sem_inc(S["tick_sp"], 1)
                    dma(wring[:, k % 2, :], w[k * P:(k + 1) * P, :], f"w{k % 2}", q)

            def out(st, T):
                yield from ()
                stream(st, "w_out")
                if st == "first":
                    e.wait_ge(dve_done, c.at("dve", "residual"))
                    e.sem_inc(S["tick_sp"], 1)
                    dma(xa[NSMP:P, :], xa[0:NSMP, :], "dup", "dup")

            def query(st, T):
                yield from ()
                stream(st, "w_query")

            def tail(st, T):
                if st == "first":
                    return
                e.wait_ge(dve_done, c.at("dve", "y"))
                e.sem_inc(S["tick_sp"], 1)
                if st == "second":
                    dma(A["o_ys"], xr[0:NSMP, :], "y_out", "y")
                else:
                    dma(A["o_yp"][bass.ds((T - 2) * P, P) if st == "loop" else slice(SEQ - P, SEQ), :], xr[:],
                        "y_out", "y")
                if st == "last":
                    st_out = A["o_rp"].rearrange("(c a) d e -> a d c e", a=2)
                    for a in range(2):
                        dma(st_out[a], state[64 * a:64 * a + 64, :, :], "st_out", f"rp{a}")
                    for s in ("kv_out", "y_out", "st_out"):
                        e.wait_ge(S[s], start(s, "last", 0) + new_counts.get((s, "last"), 0))

            run(c, dict(norm1=norm1, kv=kv, ret2=ret2, out=out, query=query), None, tail, e)

        @block.gpsimd
        def _(e):
            c = Counter(e, "pool")

            def gather(dst, table, index, s, name):
                e.indirect_dma_start(dst, None, table, bass.IndirectOffsetOnAxis(ap=index, axis=0)).then_inc(S[s], c.count(name, s, 16))

            def begin(st, T):
                if st != "first":
                    return
                e.memset(epsc[:], EPS).then_inc(pool_done, c.count())
                e.memset(xa[:], 0.0).then_inc(pool_done, c.count("x cleared"))
                e.memset(ckvR[:], 0.0).then_inc(pool_done, c.count())
                e.memset(ckvT[:], 0.0).then_inc(pool_done, c.count())
                e.memset(krT[:], 0.0).then_inc(pool_done, c.count())
                e.memset(ha[:], 0.0).then_inc(pool_done, c.count())
                e.memset(ones[:], 1.0).then_inc(pool_done, c.count("cleared"))
                pt = A["page_table"].rearrange("b g -> (b g)").partition_broadcast(P)
                e.dma_start(idx_v[:, 64:128].bitcast(I32), pt).then_inc(S["pg"], c.count("pages", "pg", 16))
                e.iota(small[:, 90:91].bitcast(I32), [[0, 1]], base=0, channel_multiplier=1).then_inc(pool_done, c.count("iota p"))

            def att(st, T, h):
                yield from ()
                if st != "first":
                    return
                if h == 0:
                    e.wait_ge(dve_done, c.at("dve", "page rows"))
                if h >= 2:
                    e.wait_ge(pe_done, c.at("pe", f"s keys used {h - 2}"))
                rows = A["cache_ckv"].rearrange("o g k c -> (o g k) c")
                krows = A["cache_krope"].rearrange("o g k c -> (o g k) c")
                dst = cachev if h % 2 == 0 else V[:, 3, :]
                for j in range(PAGES):
                    ix = idx_v[:, h * PAGES + j:h * PAGES + j + 1]
                    gather(dst[:, P * j:P * j + P], rows, ix, f"cache{h % 2}", f"c{h}{j}")
                for j in range(PAGES):
                    ix = idx_v[:, h * PAGES + j:h * PAGES + j + 1]
                    gather(krc[:, 256 * (h % 2) + ROPE * j:256 * (h % 2) + ROPE * j + ROPE], krows, ix,
                           f"cache{h % 2}", f"k{h}{j}")

            ut = A["u_experts"].rearrange("o e d -> (o e) d")
            vt = A["v_experts"].rearrange("o e d -> (o e) d")

            def peer(st, T, s):
                if RING <= s < nslots(st):
                    e.wait_ge(dve_done, c.at("dve", f"u{s - RING}"))
                    e.sem_inc(S["tick_pool"], 1)
                    gather(U[:, s % RING, :], ut, idx_u[:, s:s + 1], f"gu{s % RING}", f"u{s}")
                s -= GRP
                if s >= 0:
                    if s == 0:
                        e.wait_ge(dve_done, c.begun("dve"))
                        e.sem_inc(S["tick_pool"], 1)
                        e.wait_ge(pe_done, c.begun("pe"))
                        e.sem_inc(S["tick_pool"], 1)
                    if s >= RING:
                        e.wait_ge(pe_done, c.at("pe", f"v{s - RING}"))
                        e.sem_inc(S["tick_pool"], 1)
                    gather(V[:, s % RING, :], vt, idx_v[:, s:s + 1], f"gv{s % RING}", f"v{s}")
                    s += GRP
                    if st != "last" and s == nslots(st) + 1:
                        ahead(st)

            def ahead(st):
                e.wait_ge(dve_done, c.at("dve", "idx_u"))
                e.sem_inc(S["tick_pool"], 1)
                if st == "first":
                    e.wait_ge(pe_done, c.at("pe", "s mla"))
                for s in range(RING):
                    gather(U[:, s, :], ut, idx_u[:, s:s + 1], f"gu{s}", f"next u{s}")

            def tail(st, T):
                if st == "first":
                    ahead(st)

            run(c, dict(begin=begin, att=att), peer, tail, e)

        @block.tensor
        def _(e):
            c = Counter(e, "pe")
            mm = e.matmul

            def transposes(src, n, dst, width=P, rows=P):
                for k in range(n):
                    m = e.transpose(dst(k), src(k), ident[0:rows, 0:rows])
                return m

            def norm1(st, T):
                yield
                yield
                if st == "first":
                    e.wait_ge(S["ld_id"], c.at("ld_id", "gq"))
                e.wait_ge(act_done, c.at("act", "xn"))
                transposes(lambda k: scr[:, P * k:P * k + P], NCH, lambda k: PB[:, P * k:P * k + P]).then_inc(pe_done, c.count("xT"))

            def projection(st, T):
                for n in range(5):
                    if n:
                        yield
                    lo, hi = 512 * n, min(512 * n + 512, IN_W)
                    if st == "first":
                        e.wait_ge(S[f"win{n}"], c.at(f"win{n}", "w"))
                    if n == 0:
                        e.wait_ge(act_done, c.at("act", "xT0"))
                        e.wait_ge(dve_done, c.at("dve", "xT1"))
                    if n >= 3:
                        e.wait_ge(act_done, c.at("act", f"proj{n - 3}"))
                    for k in range(NCH):
                        m = mm(PA[:, 512 * (n % 3):512 * (n % 3) + hi - lo], T1[:, P * k:P * k + P], w_in[:, k, lo:hi],
                               start=k == 0, stop=k == NCH - 1)
                    m.then_inc(pe_done, c.count(f"proj{n}"))

            def kv(st, T):
                yield
                e.wait_ge(dve_done, c.at("dve", "krope"))
                e.wait_ge(act_done, c.at("act", "cqn"))
                e.transpose(PB[:, 0:P], ckvS[:], ident[:])
                e.transpose(PB[0:ROPE, P:2 * P], krS[:], ident[:])
                e.transpose(PB[:, 2 * P:3 * P], B1[:, 0:P], ident[:])
                e.transpose(PB[:, 3 * P:4 * P], B1[:, P:2 * P], ident[:]).then_inc(pe_done, c.count("kvT"))

            def ret1(st, T):
                e.wait_ge(dve_done, c.at("dve", "rope"))
                e.wait_ge(act_done, c.at("act", "cqT"))
                transposes(lambda k: proj[:, C_RQ + P * k:C_RQ + P * k + P], 8,
                                 lambda k: PB[:, 512 + P * k:512 + P * k + P]).then_inc(pe_done, c.count("rT"))
                yield
                yield
                e.wait_ge(act_done, c.at("act", "rT"))
                for h in range(H):
                    o = 64 * (h % 2)
                    m = mm(PA[:, P * apart(h):P * apart(h) + P], B1[o:o + 64, 512 + P * (h // 2):512 + P * (h // 2) + P],
                           B1[o:o + 64, P * (h // 2):P * (h // 2) + P], start=True, stop=True)
                m.then_inc(pe_done, c.count("inner"))
                if st == "first":
                    e.wait_ge(S["st_in"], c.at("st_in", f"s1{DEC_B - 1}"))
                    for h in range(H):
                        o = 64 * (h % 2)
                        for b in range(DEC_B):
                            at = cross_at(h) + DEC_T * b
                            m = mm(PB[0:64, at:at + DEC_T],
                                   sst[o:o + 64, b, h // 2, :],
                                   B1[o:o + 64, P * (h // 2) + DEC_T * b:P * (h // 2) + DEC_T * b + DEC_T],
                                   start=True, stop=True)
                    m.then_inc(pe_done, c.count("crossT"))
                    e.wait_ge(act_done, c.at("act", "crossT"))
                    for h in range(H):
                        m = e.transpose(PB[0:64, cross_at(h):cross_at(h) + 64], scr[0:64, 64 * h:64 * h + 64],
                                        ident[0:64, 0:64])
                    m.then_inc(pe_done, c.count("cross"))
                else:
                    for h in range(H):
                        o = 64 * (h % 2)
                        m = mm(PB[:, cross_at(h):cross_at(h) + 64], B1[o:o + 64, P * (h // 2):P * (h // 2) + P],
                               state[o:o + 64, h // 2, :], start=True, stop=True)
                    m.then_inc(pe_done, c.count("cross"))
                yield
                yield
                e.wait_ge(dve_done, c.at("dve", "innerT"))
                for h in range(H):
                    m = mm(PB[:, 64 * h:64 * h + 64], PP[:, P * apart(h):P * apart(h) + P],
                           proj[:, C_RV + 64 * h:C_RV + 64 * h + 64], start=True, stop=True)
                m.then_inc(pe_done, c.count("o1"))

            def ret2(st, T):
                yield from ()
                for b in range(DEC_B + 1) if st == "first" else [0]:
                    e.wait_ge(dve_done, c.at("dve", f"kd{b}"))
                    o = 512 * (b % 2)
                    if st != "first":
                        o = 0
                    if b >= 2:
                        e.wait_ge(dve_done, c.at("dve", f"sn{b - 2}"))
                    for q in range(4):
                        m = mm(PA[:, o + P * q:o + P * q + P],
                               (scr[:, 512 + P * q:512 + P * q + P] if st != "first" else
                                kdb[:, 512 * (b % 2) + P * q:512 * (b % 2) + P * q + P]),
                               proj[:, C_RV + P * q:C_RV + P * q + P], start=True, stop=True)
                    m.then_inc(pe_done, c.count(f"su{b}"))

            def q1(st, T):
                if st == "first":
                    e.wait_ge(S["ld_w"], c.at("ld_w", "all"))
                e.wait_ge(dve_done, c.at("dve", "ret"))
                for n in range(2):
                    for k in range(2):
                        m = mm(PA[:, 512 * n:512 * n + 384], ckq(k), w_uq[:, k, 384 * n:384 * n + 384],
                               start=k == 0, stop=k == 1)
                m.then_inc(pe_done, c.count("q"))
                yield
                e.wait_ge(act_done, c.at("act", "q rope in"))
                transposes(lambda k: scr[:, P * k:P * k + P], 4, lambda k: PB[:, P * k:P * k + P]).then_inc(pe_done, c.count("qnT"))
                yield
                e.wait_ge(dve_done, c.at("dve", "q rope"))
                for h in range(H):
                    m = e.transpose(PB[0:ROPE, 512 + P * h:512 + P * h + P],
                                    scr[:, 512 + ROPE * h:512 + ROPE * h + ROPE], ident[:])
                m.then_inc(pe_done, c.count("qrT"))
                yield
                e.wait_ge(act_done, c.at("act", "qnT"))
                for h in range(H):
                    o = 64 * (h % 2)
                    m = mm(PA[:, P * apart(h):P * apart(h) + P], ukT[o:o + 64, h // 2, :],
                           PP[o:o + 64, P * (h // 2):P * (h // 2) + P], start=True, stop=True)
                m.then_inc(pe_done, c.count("qlat"))

            def ckq(k):
                return T1[:, P * k:P * k + P]

            def att_sample(h):
                rows = cachev if h % 2 == 0 else V[:, 3, :]
                kro = 256 * (h % 2)
                e.wait_ge(S["cache" + str(h % 2)], c.at("cache" + str(h % 2), f"k{h}7"))
                if h == 0:
                    e.wait_ge(act_done, c.at("act", "qlat"))
                    e.wait_ge(act_done, c.at("act", "qrT"))
                else:
                    e.wait_ge(dve_done, c.at("dve", f"s pT1 {h - 1}"))
                    e.wait_ge(act_done, c.at("act", f"s lat {h - 1}"))
                transposes(lambda k: rows[:, P * k:P * k + P], 8, lambda k: PB[:, P * k:P * k + P]).then_inc(pe_done, c.count(f"s kT {h}"))
                for k in range(PAGES):
                    m = e.transpose(PA[0:ROPE, P * k:P * k + P], krc[:, kro + ROPE * k:kro + ROPE * k + ROPE], ident[:])
                m.then_inc(pe_done, c.count(f"s krT {h}"))
                e.wait_ge(act_done, c.at("act", f"s kT {h}"))
                e.wait_ge(dve_done, c.at("dve", f"s krT {h}"))
                t0 = DEC_T * h
                qn = B1[:, t0 * H:t0 * H + 64]
                qr = T1[0:ROPE, t0 * H:t0 * H + 64]
                for n in range(2):
                    mm(PA[0:64, 512 * n:512 * n + 512], qn, kcT[:, 512 * n:512 * n + 512], start=True, stop=False)
                    mm(PA[0:64, 512 * n:512 * n + 512], qr, krcT[0:ROPE, 512 * n:512 * n + 512], start=False, stop=True)
                mm(PA[0:64, 1024:1152], qn, ckvT[:, SEQ:NKEY], start=True, stop=False)
                mm(PA[0:64, 1024:1152], qr, krT[:, SEQ:NKEY], start=False, stop=True).then_inc(pe_done, c.count(f"s S {h}"))
                e.wait_ge(dve_done, c.at("dve", f"s p {h}"))
                for k in range(NKC):
                    m = e.transpose(PB[:, P * k:P * k + 64], PP[0:64, P * k:P * k + P], ident[0:64, 0:64])
                m.then_inc(pe_done, c.count(f"s pT {h}"))
                e.wait_ge(act_done, c.at("act", f"s pT0 {h}"))
                e.wait_ge(dve_done, c.at("dve", f"s pT1 {h}"))
                for k in range(NKC):
                    m = mm(PB[:, 0:64], rows[:, P * k:P * k + P] if k < 8 else ckvR[:, SEQ:NKEY],
                           scr[:, P * k:P * k + 64], start=k == 0, stop=k == NKC - 1)
                m.then_inc(pe_done, c.count(f"s keys used {h}"))
                if h == DEC_B - 1:
                    e.wait_ge(act_done, c.at("act", f"s lat {h}"))
                    for k in range(H):
                        m = mm(PA[0:64, VD * k:VD * k + VD], latS[:, 64 * k:64 * k + 64], w_uv[:, VD * k:VD * k + VD],
                               start=True, stop=True)
                    m.then_inc(pe_done, c.count("s mla"))

            def scores(h):
                for lo, hi in ((0, 512), (512, 1024), (1024, 1152)):
                    mm(PA[:, lo:hi], B1[:, P * h:P * h + P], ckvT[:, lo:hi], start=True, stop=False)
                    m = mm(PA[:, lo:hi], T1[0:ROPE, P * h:P * h + P], krT[:, lo:hi], start=False, stop=True)
                return m

            def latent(h):
                e.wait_ge(act_done, c.at("act", f"pT0 {h}"))
                e.wait_ge(dve_done, c.at("dve", f"pT1 {h}"))
                for k in range(NKC):
                    m = mm(PB[:, 0:P], ckvR[:, P * k:P * k + P], scr[:, P * k:P * k + P], start=k == 0,
                           stop=k == NKC - 1)
                m.then_inc(pe_done, c.count(f"lat{h}"))

            def values(h):
                e.wait_ge(act_done, c.at("act", f"lat{h}"))
                mm(PB[:, 512:512 + VD], latT[:], w_uv[:, VD * h:VD * h + VD], start=True,
                   stop=True).then_inc(pe_done, c.count(f"mla{h}"))

            def att(st, T, h):
                if st == "first":
                    att_sample(h)
                    return
                if h == 0:
                    e.wait_ge(act_done, c.at("act", "qlat"))
                    e.wait_ge(S["const"], c.at("const", "all"))
                else:
                    e.wait_ge(dve_done, c.at("dve", f"nb{h - 1}"))
                scores(h).then_inc(pe_done, c.count(f"S{h}"))
                yield
                if h:
                    latent(h - 1)
                yield
                if h:
                    values(h - 1)
                yield
                e.wait_ge(act_done, c.at("act", f"p{h}"))
                if h:
                    e.wait_ge(act_done, c.at("act", f"mla{h - 1}"))
                transposes(lambda k: PP[:, P * k:P * k + P], NKC,
                           lambda k: PB[:, P * k:P * k + P]).then_inc(pe_done, c.count(f"pT{h}"))

            def attend(st, T):
                if st == "first":
                    return
                yield
                latent(H - 1)
                yield
                values(H - 1)

            def out(st, T):
                if st == "first":
                    e.wait_ge(act_done, c.at("act", "s mla"))
                else:
                    e.wait_ge(act_done, c.at("act", f"mla{H - 1}"))
                transposes(lambda k: cat[:, P * k:P * k + P], NCH, lambda k: PB[:, P * k:P * k + P]).then_inc(pe_done, c.count("catT"))
                yield
                yield
                e.wait_ge(act_done, c.at("act", "catT0"))
                e.wait_ge(dve_done, c.at("dve", "catT1"))
                for k in range(NCH):
                    e.wait_ge(S[f"w{k % 2}"], c.at(f"w{k % 2}", f"o{k}"))
                    for n in range(2):
                        m = mm(PA[:, 512 * n:512 * n + 512], T1[:, P * k:P * k + P], wring[:, k % 2, 512 * n:512 * n + 512],
                               start=k == 0, stop=k == NCH - 1)
                    m.then_inc(pe_done, c.count(f"used o{k}"))
                    if k == 3:
                        yield

            def gain_rows(row, dst):
                for n in range(2):
                    m = mm(dst[:, 512 * n:512 * n + 512], ones[row:row + 1, :], gains[row:row + 1, 512 * n:512 * n + 512],
                           start=True, stop=True)
                return m

            def norm2(st, T):
                if st == "first":
                    e.wait_ge(S["const"], c.at("const", "all"))
                    e.wait_ge(pool_done, c.at("pool", "cleared"))
                gain_rows(0, PB).then_inc(pe_done, c.count("gffn"))
                yield
                e.wait_ge(dve_done, c.at("dve", "h"))
                transposes(lambda k: ha[:, P * k:P * k + P], NCH, lambda k: PA[:, P * k:P * k + P]).then_inc(pe_done, c.count("hT"))

            def query(st, T):
                e.wait_ge(act_done, c.at("act", "hT0"))
                e.wait_ge(dve_done, c.at("dve", "hT1"))
                for k in range(NCH):
                    e.wait_ge(S[f"w{k % 2}"], c.at(f"w{k % 2}", f"q{k}"))
                    for h in range(H):
                        m = mm(PB[:, P * h:P * h + P], wring[:, k % 2, P * h:P * h + P], T1[:, P * k:P * k + P],
                               start=k == 0 and h % 4 == 0, stop=k == NCH - 1, skip_group_check=True)
                    m.then_inc(pe_done, c.count(f"used q{k}"))
                    if k in (3, 7):
                        yield
                yield
                e.wait_ge(act_done, c.at("act", "qT"))
                for h in range(H):
                    dst = PA if h < 4 else PB
                    for p in range(2):
                        o = P * (4 * p + h % 4)
                        m = mm(dst[:, o:o + P], scr[64 * p:64 * p + 64, P * h:P * h + P],
                               keysT[64 * p:64 * p + 64, h, :], start=True, stop=True)
                    if h % 4 == 3:
                        m.then_inc(pe_done, c.count(f"sc{h // 4}"))

            def peer(st, T, s):
                s -= GRP
                if s < 0:
                    return
                e.wait_ge(S[f"gv{s % RING}"], c.at(f"gv{s % RING}", f"v{s}"))
                e.wait_ge(dve_done, c.at("dve", f"d{s}"))
                for q in range(2):
                    m = mm(Y[:, 512 * q:512 * q + 512], diag[:, s % RING, :], V[:, s % RING, 512 * q:512 * q + 512],
                           start=s == 0, stop=s == nslots(st) - 1, skip_group_check=True)
                m.then_inc(pe_done, c.count(f"v{s}"))

            def tail(st, T):
                if st == "first":
                    e.wait_ge(act_done, c.at("act", "sc1"))
                    return
                e.wait_ge(act_done, c.at("act", "y sq"))
                gain_rows(32, Y).then_inc(pe_done, c.count("gfin"))

            run(c, dict(norm1=norm1, proj=projection, kv=kv, ret1=ret1, ret2=ret2, q1=q1, att=att, out=out,
                        norm2=norm2, query=query, attend=attend), peer, tail, e)

        @block.scalar
        def _(e):
            c = Counter(e, "act")
            act = e.activation

            def by_half(x):
                return x.rearrange("p (q s t) -> p s q t", q=4, s=2)

            def root(dst, ss, n, name):
                e.wait_ge(act_done, c.here())
                act(dst, ss, ACT.Sqrt, bias=epsc[:], scale=1.0 / n).then_inc(act_done, c.count(name))

            def norm1(st, T):
                yield
                if st == "first":
                    e.wait_ge(S["ld_id"], c.at("ld_id", "gq"))
                e.wait_ge(S["x_in"], c.at("x_in", "x"))
                act(scr[:, 0:D], xa[:], ACT.Square, accum_out=small[:, 0:1]).then_inc(act_done, c.count())
                root(small[:, 1:2], small[:, 0:1], D, "x sq")
                e.wait_ge(dve_done, c.at("dve", "x rstd"))
                e.wait_ge(act_done, c.here())
                act(scr[:, 0:D], xa[:], ACT.Copy, scale=small[:, 1:2]).then_inc(act_done, c.count("xn"))
                yield
                yield
                e.wait_ge(pe_done, c.at("pe", "xT"))
                for k in range(4):
                    act(T1[:, P * k:P * k + P], PB[:, P * k:P * k + P], ACT.Copy, scale=gcol[:, k:k + 1]).then_inc(act_done, c.count("xT0" if k == 3 else None))

            def projection(st, T):
                for n in range(5):
                    if n:
                        yield
                    lo, hi = 512 * n, min(512 * n + 512, IN_W)
                    e.wait_ge(pe_done, c.at("pe", f"proj{n}"))
                    act(proj[:, lo:hi], PA[:, 512 * (n % 3):512 * (n % 3) + hi - lo], ACT.Copy).then_inc(act_done, c.count(f"proj{n}"))

            def kv(st, T):
                e.wait_ge(act_done, c.here())
                act(scr[:, 0:Q_LORA], proj[:, 0:Q_LORA], ACT.Square, accum_out=small[:, 2:3]).then_inc(act_done, c.count())
                act(scr[:, C_KV:C_KV + KV], proj[:, C_KV:C_KV + KV], ACT.Square, accum_out=small[:, 3:4]).then_inc(act_done, c.count())
                root(small[:, 4:5], small[:, 2:3], Q_LORA, None)
                root(small[:, 5:6], small[:, 3:4], KV, "kv sq")
                e.wait_ge(dve_done, c.at("dve", "kv rstd"))
                act(B1[:, 0:Q_LORA], proj[:, 0:Q_LORA], ACT.Copy, scale=small[:, 4:5]).then_inc(act_done, c.count("cqn"))
                at = SEQ if st == "first" else (T - 1) * P
                e.wait_ge(dve_done, c.at("dve", "krope"))
                act(ckvR[:, bass.ds(at, P)], ckvS[:], ACT.Copy).then_inc(act_done, c.count())
                yield
                yield
                e.wait_ge(pe_done, c.at("pe", "kvT"))
                act(ckvT[:, bass.ds(at, P)], PB[:, 0:P], ACT.Copy).then_inc(act_done, c.count())
                act(krT[:, bass.ds(at, P)], PB[0:ROPE, P:2 * P], ACT.Copy).then_inc(act_done, c.count())
                for k in range(2):
                    act(T1[:, P * k:P * k + P], PB[:, P * (2 + k):P * (3 + k)], ACT.Copy, scale=gq[:, k:k + 1]).then_inc(act_done, c.count("cqT" if k else None))

            def ret1(st, T):
                yield
                e.wait_ge(pe_done, c.at("pe", "rT"))
                act(B1[:], PB[:, 512:1536], ACT.Copy).then_inc(act_done, c.count("rT"))
                if st == "first":
                    e.wait_ge(pe_done, c.at("pe", "crossT"))
                    act(by_half(scr[0:64, 0:512]),
                              PB[0:64, 512:1536].rearrange("p (s x) -> p s x", s=2)[:, :, 0:256]
                              .rearrange("p s (q t) -> p s q t", q=4), ACT.Copy).then_inc(act_done, c.count("crossT"))
                yield
                yield
                yield
                yield
                e.wait_ge(dve_done, c.at("dve", "o"))
                act(PP[:, 0:512], scr[:, 0:512], ACT.Square).then_inc(act_done, c.count("o sq"))
                act(PP[:, 512:1024], proj[:, C_RG:C_RG + 512], ACT.Exp, scale=-1.0).then_inc(act_done, c.count("exp rg"))

            def ret2(st, T):
                yield
                e.wait_ge(dve_done, c.at("dve", "hn ss"))
                root(small[:, 8:16], small[:, 8:16], 64, "hn")

            def q1(st, T):
                e.wait_ge(pe_done, c.at("pe", "q"))
                for n in range(2):
                    src = PA[:, 512 * n:512 * n + 384].rearrange("p (h d) -> p h d", d=96)
                    act(scr[:, 256 * n:256 * n + 256].rearrange("p (h d) -> p h d", d=64), src[:, :, 0:64],
                              ACT.Copy).then_inc(act_done, c.count())
                    act(scr[:, 512 + 128 * n:640 + 128 * n].rearrange("p (h d) -> p h d", d=32),
                              src[:, :, 64:96], ACT.Copy).then_inc(act_done, c.count("q rope in" if n else None))
                yield
                e.wait_ge(pe_done, c.at("pe", "qnT"))
                act(PP[:, 0:512], PB[:, 0:512], ACT.Copy).then_inc(act_done, c.count("qnT"))
                yield
                e.wait_ge(pe_done, c.at("pe", "qrT"))
                if st == "first":
                    act(T1[0:ROPE, :].rearrange("p (t h) -> p h t", h=H),
                              PB[0:ROPE, 512:1536].rearrange("p (h t) -> p h t", h=H), ACT.Copy).then_inc(act_done, c.count("qrT"))
                else:
                    act(T1[0:ROPE, :], PB[0:ROPE, 512:1536], ACT.Copy).then_inc(act_done, c.count("qrT"))
                yield
                e.wait_ge(pe_done, c.at("pe", "qlat"))
                dst = B1[:].rearrange("p (t q s) -> p s q t" if st == "first" else "p (q s t) -> p s q t", q=4, s=2)
                act(dst, PA[:, 0:1024].rearrange("p (s q t) -> p s q t", s=2, q=4), ACT.Copy).then_inc(act_done, c.count("qlat"))

            def att_sample(h):
                e.wait_ge(pe_done, c.at("pe", f"s kT {h}"))
                act(kcT, PB[:, 0:1024], ACT.Copy).then_inc(act_done, c.count(f"s kT {h}"))
                e.wait_ge(dve_done, c.at("dve", f"s nb {h}"))
                act(PP[0:64, :], PP[0:64, :], ACT.Exp, bias=small[0:64, 21:22], scale=SCALE,
                          accum_out=small[0:64, 22:23]).then_inc(act_done, c.count(f"s p {h}"))
                e.wait_ge(pe_done, c.at("pe", f"s pT {h}"))
                act(scr[:, 0:1024].rearrange("p (k r) -> p k r", r=P)[:, :, 0:64],
                          PB[:, 0:1024].rearrange("p (k r) -> p k r", r=P)[:, :, 0:64], ACT.Copy).then_inc(act_done, c.count(f"s pT0 {h}"))
                e.wait_ge(pe_done, c.at("pe", f"s keys used {h}"))
                act(latS.rearrange("p (h t) -> p h t", h=H)[:, :, DEC_T * h:DEC_T * h + DEC_T],
                          PB[:, 0:64].rearrange("p (t h) -> p h t", h=H), ACT.Copy).then_inc(act_done, c.count(f"s lat {h}"))
                if h == DEC_B - 1:
                    e.wait_ge(pe_done, c.at("pe", "s mla"))
                    act(cat[0:64, 0:512], PA[0:64, 0:512], ACT.Copy).then_inc(act_done, c.count("s mla"))

            def turned(h):
                e.wait_ge(pe_done, c.at("pe", f"pT{h}"))
                act(scr[:, 0:1024], PB[:, 0:1024], ACT.Copy).then_inc(act_done, c.count(f"pT0 {h}"))

            def latent(h):
                e.wait_ge(pe_done, c.at("pe", f"lat{h}"))
                act(latT[:], PB[:, 0:P], ACT.Copy).then_inc(act_done, c.count(f"lat{h}"))

            def values(h):
                e.wait_ge(pe_done, c.at("pe", f"mla{h}"))
                act(cat[:, VD * h:VD * h + VD], PB[:, 512:512 + VD], ACT.Copy,
                    scale=small[:, 40 + h:41 + h]).then_inc(act_done, c.count(f"mla{h}"))

            def att(st, T, h):
                if st == "first":
                    att_sample(h)
                    return
                if h:
                    turned(h - 1)
                yield
                e.wait_ge(dve_done, c.at("dve", f"nb{h}"))
                act(PP[:], PP[:], ACT.Exp, bias=small[:, 21:22], scale=SCALE,
                    accum_out=small[:, 48 + h:49 + h]).then_inc(act_done, c.count(f"p{h}"))
                if h:
                    latent(h - 1)
                yield
                if h:
                    e.wait_ge(dve_done, c.at("dve", f"rl{h - 1}"))
                    values(h - 1)

            def attend(st, T):
                if st == "first":
                    return
                turned(H - 1)
                yield
                latent(H - 1)
                yield
                e.wait_ge(dve_done, c.at("dve", f"rl{H - 1}"))
                values(H - 1)

            def out(st, T):
                yield
                e.wait_ge(pe_done, c.at("pe", "catT"))
                act(T1[:, 0:512], PB[:, 0:512], ACT.Copy).then_inc(act_done, c.count("catT0"))

            def norm2(st, T):
                yield from ()
                e.wait_ge(dve_done, c.at("dve", "residual"))
                if st == "first":
                    e.wait_ge(S["dup"], c.at("dup", "dup"))
                act(scr[:, 0:D], xa[:], ACT.Square, accum_out=small[:, 24:25]).then_inc(act_done, c.count())
                root(small[:, 25:26], small[:, 24:25], D, "x2 sq")
                yield
                yield
                e.wait_ge(pe_done, c.at("pe", "hT"))
                act(T1[:, 0:512], PA[:, 0:512], ACT.Copy).then_inc(act_done, c.count("hT0"))

            def query(st, T):
                yield
                yield
                e.wait_ge(pe_done, c.at("pe", f"used q{NCH - 1}"))
                act(scr[:, 0:D], PB[:, 0:D], ACT.Copy).then_inc(act_done, c.count("qT"))
                yield
                yield
                e.wait_ge(pe_done, c.at("pe", "sc0"))
                act(proj[:, 0:1024], PA[:, 0:1024], ACT.Copy).then_inc(act_done, c.count("sc0"))
                e.wait_ge(pe_done, c.at("pe", "sc1"))
                act(proj[:, 1024:2048], PB[:, 0:1024], ACT.Copy).then_inc(act_done, c.count("sc1"))

            def top3(st, T):
                yield
                e.wait_ge(dve_done, c.at("dve", "best - max"))
                act(T1[:, 256:384], T1[:, 256:384], ACT.Exp).then_inc(act_done, c.count("gate exp"))

            def peer(st, T, s):
                if s % GRP != GRP - 1 or s >= nslots(st):
                    return
                g = s // GRP
                e.wait_ge(dve_done, c.at("dve", f"u{s}"))
                if g >= 2:
                    e.wait_ge(dve_done, c.at("dve", f"d{(g - 1) * GRP - 1}"))
                act(acts[:, g % 2, :], dots[:, g % 2, :], ACT.Gelu).then_inc(act_done, c.count(f"gelu{g}"))
                if s == nslots(st) - 1 and st != "last":
                    handover(st)

            def handover(st):
                e.wait_ge(dve_done, c.at("dve", "idx_u"))
                act(hr[:], ha[:], ACT.Copy).then_inc(act_done, c.count("hr"))

            def begin(st, T):
                if st != "first":
                    if st != "second":
                        e.wait_ge(S["y_out"], c.begun("y_out"))
                    act(xr[:], xa[:], ACT.Copy).then_inc(act_done, c.count("xr"))

            def tail(st, T):
                if st == "first":
                    handover(st)
                else:
                    e.wait_ge(dve_done, c.at("dve", "y sum"))
                    act(Y, xr[:], ACT.Square, accum_out=peerv[:, 0:1]).then_inc(act_done, c.count())
                    root(peerv[:, 1:2], peerv[:, 0:1], D, "y sq")

            run(c, dict(begin=begin, norm1=norm1, proj=projection, kv=kv, ret1=ret1, ret2=ret2, q1=q1, att=att, out=out,
                        norm2=norm2, query=query, top3=top3, attend=attend), peer, tail, e)

        @block.vector
        def _(e):
            c = Counter(e, "dve")
            tt, ts, stt, red = e.tensor_tensor, e.tensor_scalar, e.scalar_tensor_tensor, e.tensor_reduce

            def invert(x, name=None):
                e.reciprocal(x, x).then_inc(dve_done, c.count(name))

            def settle():
                e.wait_ge(dve_done, c.here())
                e.sem_inc(S["tick_dve"], 1)

            def norm1(st, T):
                yield
                if st == "first":
                    e.wait_ge(pool_done, c.at("pool", "iota p"))
                    e.wait_ge(S["pg"], c.at("pg", "pages"))
                    e.tensor_copy(small[:, 91:92], small[:, 90:91].bitcast(I32)).then_inc(dve_done, c.count())
                    pf = ha[:, 0:64]
                    e.wait_ge(pool_done, c.at("pool", "cleared"))
                    e.tensor_copy(PP[:, 0:64], idx_v[:, 64:128].bitcast(I32)).then_inc(dve_done, c.count())
                    e.wait_ge(dve_done, c.here())
                    ts(PP[:, 0:64], PP[:, 0:64], float(P), small[:, 91:92], ALU.mult, ALU.add).then_inc(dve_done, c.count())
                    e.wait_ge(dve_done, c.here())
                    e.tensor_copy(idx_v[:, 0:64], PP[:, 0:64]).then_inc(dve_done, c.count("page rows"))
                    e.wait_ge(S["ld_id"], c.at("ld_id", "gq"))
                e.wait_ge(act_done, c.at("act", "x sq"))
                invert(small[:, 1:2], "x rstd")
                yield
                yield
                e.wait_ge(pe_done, c.at("pe", "xT"))
                for k in range(4, 8):
                    ts(T1[:, P * k:P * k + P], PB[:, P * k:P * k + P], gcol[:, k:k + 1], None, ALU.mult).then_inc(dve_done, c.count("xT1" if k == 7 else None))

            def rotate(x, n, half, cos, sin, tmpa, tmpb, name):
                xv = x.rearrange("p (n s f) -> p n s f", n=n, s=2)
                a = tmpa.rearrange("p (n s f) -> p n s f", n=n, s=2)
                b = tmpb.rearrange("p (n s f) -> p n s f", n=n, s=2)
                cb = cos.unsqueeze(1).to_broadcast([P, n, half])
                sbc = sin.unsqueeze(1).to_broadcast([P, n, half])
                for s in range(2):
                    tt(a[:, :, s, :], xv[:, :, s, :], cb, ALU.mult).then_inc(dve_done, c.count())
                    tt(b[:, :, s, :], xv[:, :, 1 - s, :], sbc, ALU.mult).then_inc(dve_done, c.count())
                e.wait_ge(dve_done, c.here())
                tt(xv[:, :, 0, :], a[:, :, 0, :], b[:, :, 0, :], ALU.subtract).then_inc(dve_done, c.count())
                tt(xv[:, :, 1, :], a[:, :, 1, :], b[:, :, 1, :], ALU.add).then_inc(dve_done, c.count(name))

            cos32, sin32 = trig[:, 0:32], trig[:, 32:64]
            cos16, sin16 = trig2[:, 0, :, 0], trig2[:, 1, :, 0]

            def kv(st, T):
                e.wait_ge(S["const"], c.at("const", "all"))
                e.wait_ge(act_done, c.at("act", "kv sq"))
                invert(small[:, 4:6], "kv rstd")
                e.tensor_copy(krS[:], proj[:, C_KR:C_KR + ROPE]).then_inc(dve_done, c.count())
                e.wait_ge(dve_done, c.here())
                stt(ckvS[:], proj[:, C_KV:C_KV + KV], small[:, 5:6], gkv[:], ALU.mult, ALU.mult).then_inc(dve_done, c.count())
                rotate(krS[:], 1, 16, cos16, sin16, PP[:, 0:32], PP[:, 32:64], "krope")
                yield
                e.wait_ge(dve_done, c.here())
                rotate(proj[:, C_RQ:C_RV], 16, 32, cos32, sin32, scr[:, 0:1024], PP[:, 0:1024], "rope")

            def by_half(x):
                return x.rearrange("p (q s e) -> p s q e", q=4, s=2)

            hb = lambda x: x.unsqueeze(2).to_broadcast([x.shape[0], H, 64])
            hv = lambda x: x.rearrange("p (h d) -> p h d", h=H)

            def ret1(st, T):
                e.wait_ge(dve_done, c.here())
                tt(hv(scr[:, 512:1024]), hv(proj[:, C_RK:C_RK + 512]), hb(kdecc), ALU.mult).then_inc(dve_done, c.count("kd0" if st != "first" else None))
                yield
                yield
                yield
                e.wait_ge(pe_done, c.at("pe", "inner"))
                tt(PP[:, 0:1024].rearrange("p (h i) -> p h i", h=H), PA[:, 0:1024].rearrange("p (h i) -> p h i", h=H),
                         dmat[:], ALU.mult).then_inc(dve_done, c.count("innerT"))
                e.wait_ge(pe_done, c.at("pe", "cross"))
                n = 64 if st == "first" else P
                for a in range(2):
                    src = PB[0:n, 512 + 512 * a:768 + 512 * a].rearrange("p (q e) -> p q e", q=4)
                    f = crossc[0:n, :].rearrange("p (q s) -> p s q", s=2)[:, a, :].unsqueeze(2).to_broadcast([n, 4, 64])
                    tt(by_half(scr[0:n, 0:512])[:, a, :, :], src, f, ALU.mult).then_inc(dve_done, c.count())
                yield
                yield
                e.wait_ge(pe_done, c.at("pe", "o1"))
                e.wait_ge(dve_done, c.here())
                if st == "first":
                    e.tensor_copy(scr[64:P, 0:512], PB[64:P, 0:512]).then_inc(dve_done, c.count())
                tt(scr[0:n, 0:512], PB[0:n, 0:512], scr[0:n, 0:512], ALU.add).then_inc(dve_done, c.count("o"))

            def ret2(st, T):
                gb = lambda x, m: x.unsqueeze(1).unsqueeze(3).to_broadcast([P, m, 4, 64])
                if st == "first":
                    e.wait_ge(dve_done, c.here())
                    for b in range(DEC_B + 1):
                        if b < DEC_B:
                            tt(sst[:, b, :, :], sst[:, b, :, :], gchunk.unsqueeze(2).to_broadcast([P, 4, 64]),
                                     ALU.mult).then_inc(dve_done, c.count())
                        if b >= 2:
                            e.wait_ge(pe_done, c.at("pe", f"su{b - 2}"))
                        ts(kdb[:, 512 * (b % 2):512 * (b % 2) + 512], scr[:, 512:1024], onehot[:, b:b + 1], None,
                                 ALU.mult).then_inc(dve_done, c.count(f"kd{b}"))
                        if b >= 1:
                            add_states(b - 1)
                    add_states(DEC_B)
                else:
                    yield
                    e.wait_ge(pe_done, c.at("pe", "su0"))
                    tt(state[:], state[:], gchunk.unsqueeze(2).to_broadcast([P, 4, 64]), ALU.mult).then_inc(dve_done, c.count())
                    e.wait_ge(dve_done, c.here())
                    for a in range(2):
                        r = slice(64 * a, 64 * a + 64)
                        up = PA[r, 0:512].rearrange("p (q e) -> p q e", q=4)[:, :, 64 * a:64 * a + 64]
                        tt(state[r, :, :], up, state[r, :, :], ALU.add).then_inc(dve_done, c.count())
                e.wait_ge(act_done, c.at("act", "exp rg"))
                e.wait_ge(dve_done, c.here())
                red(small[:, 8:16], hv(PP[:, 0:512]), AX, ALU.add).then_inc(dve_done, c.count("hn ss"))
                ts(PP[:, 512:1024], PP[:, 512:1024], 1.0, None, ALU.add).then_inc(dve_done, c.count())
                e.wait_ge(dve_done, c.here())
                e.reciprocal(PP[:, 512:1024], PP[:, 512:1024]).then_inc(dve_done, c.count())
                yield
                e.wait_ge(act_done, c.at("act", "hn"))
                invert(small[:, 8:16])
                e.wait_ge(dve_done, c.here())
                tt(PP[:, 512:1024], PP[:, 512:1024], proj[:, C_RG:C_RG + 512], ALU.mult).then_inc(dve_done, c.count())
                tt(hv(scr[:, 0:512]), hv(scr[:, 0:512]), hb(small[:, 8:16]), ALU.mult).then_inc(dve_done, c.count())
                e.wait_ge(dve_done, c.here())
                if st == "first":
                    e.wait_ge(pool_done, c.at("pool", "cleared"))
                tt(cat[:, 512:1024], scr[:, 0:512], PP[:, 512:1024], ALU.mult).then_inc(dve_done, c.count("ret"))

            def add_states(b):
                e.wait_ge(pe_done, c.at("pe", f"su{b}"))
                e.wait_ge(dve_done, c.here())
                for a in range(2):
                    r = slice(64 * a, 64 * a + 64)
                    up = PA[r, 512 * (b % 2):512 * (b % 2) + 512].rearrange("p (q e) -> p q e", q=4)[:, :, 64 * a:64 * a + 64]
                    if b < DEC_B:
                        tt(sst[r, b, :, :], up, sst[r, b, :, :], ALU.add).then_inc(dve_done, c.count(None if a == 0 else f"sn{b}"))
                    else:
                        e.tensor_copy(state[r, :, :], up).then_inc(dve_done, c.count("states" if a else None))

            def q1(st, T):
                yield
                e.wait_ge(act_done, c.at("act", "q rope in"))
                e.wait_ge(dve_done, c.here())
                rotate(scr[:, 512:768], H, 16, cos16, sin16, PP[:, 512:768], PP[:, 768:1024], "q rope")

            def att_sample(h):
                e.wait_ge(pe_done, c.at("pe", f"s krT {h}"))
                e.tensor_copy(krcT[0:ROPE, :], PA[0:ROPE, 0:1024]).then_inc(dve_done, c.count(f"s krT {h}"))
                e.wait_ge(pe_done, c.at("pe", f"s S {h}"))
                e.tensor_copy(PP[0:64, 0:1024], PA[0:64, 0:1024]).then_inc(dve_done, c.count())
                lo = 120 - DEC_T * h
                tt(PP[0:64, 1024:1152], PA[0:64, 1024:1152], newm[:, lo:lo + P], ALU.add).then_inc(dve_done, c.count())
                e.wait_ge(dve_done, c.here())
                red(small[0:64, 20:21], PP[0:64, :], AX, ALU.max).then_inc(dve_done, c.count())
                e.wait_ge(dve_done, c.here())
                ts(small[0:64, 21:22], small[0:64, 20:21], -SCALE, None, ALU.mult).then_inc(dve_done, c.count(f"s nb {h}"))
                e.wait_ge(act_done, c.at("act", f"s p {h}"))
                e.reciprocal(small[0:64, 23:24], small[0:64, 22:23]).then_inc(dve_done, c.count())
                e.wait_ge(dve_done, c.here())
                ts(PP[0:64, :], PP[0:64, :], small[0:64, 23:24], None, ALU.mult).then_inc(dve_done, c.count(f"s p {h}"))
                e.wait_ge(pe_done, c.at("pe", f"s pT {h}"))
                e.tensor_copy(scr[:, 1024:1088], PB[:, 1024:1088]).then_inc(dve_done, c.count(f"s pT1 {h}"))

            def turned(h):
                e.wait_ge(pe_done, c.at("pe", f"pT{h}"))
                e.tensor_copy(scr[:, 1024:1152], PB[:, 1024:1152]).then_inc(dve_done, c.count(f"pT1 {h}"))

            def att(st, T, h):
                if st == "first":
                    att_sample(h)
                    return
                if h:
                    turned(h - 1)
                yield
                e.wait_ge(pe_done, c.at("pe", f"S{h}"))
                e.sem_inc(S["tick_dve"], 1)
                e.tensor_tensor_reduce(PP[:], PA[:, 0:NKEY], mask, 1.0, NEG, ALU.add, ALU.max,
                                       small[:, 20:21]).then_inc(dve_done, c.count())
                e.wait_ge(dve_done, c.here())
                ts(small[:, 21:22], small[:, 20:21], -SCALE, None, ALU.mult).then_inc(dve_done, c.count(f"nb{h}"))
                yield
                e.wait_ge(act_done, c.at("act", f"p{h}"))
                e.reciprocal(small[:, 40 + h:41 + h], small[:, 48 + h:49 + h]).then_inc(dve_done, c.count(f"rl{h}"))

            def attend(st, T):
                if st != "first":
                    turned(H - 1)
                yield

            def out(st, T):
                yield
                e.wait_ge(pe_done, c.at("pe", "catT"))
                e.tensor_copy(T1[:, 512:1024], PB[:, 512:1024]).then_inc(dve_done, c.count("catT1"))
                yield
                yield
                yield
                e.wait_ge(pe_done, c.at("pe", f"used o{NCH - 1}"))
                tt(xa[:], PA[:, 0:D], xa[:], ALU.add).then_inc(dve_done, c.count("residual"))

            def norm2(st, T):
                e.wait_ge(act_done, c.at("act", "x2 sq"))
                invert(small[:, 25:26])
                e.wait_ge(pe_done, c.at("pe", "gffn"))
                e.wait_ge(dve_done, c.here())
                stt(ha[:], xa[:], small[:, 25:26], PB[:, 0:D], ALU.mult, ALU.mult).then_inc(dve_done, c.count("h"))
                yield
                yield
                e.wait_ge(pe_done, c.at("pe", "hT"))
                e.tensor_copy(T1[:, 512:1024], PA[:, 512:1024]).then_inc(dve_done, c.count("hT1"))

            NL = 2 * H
            val = B1[:, 0:256].rearrange("p (l k) -> p l k", l=NL)
            ival = B1[:, 256:512].bitcast(U32).rearrange("p (l k) -> p l k", l=NL)
            fval = B1[:, 512:768].rearrange("p (h s k) -> p h s k", h=H, s=2)
            valp = B1[:, 0:256].rearrange("p (h s k) -> p h s k", h=H, s=2)
            cnd = PP[:, 0:H * NPAIR].rearrange("p (h c) -> p h c", h=H)
            cnde = PP[:, H * NPAIR:2 * H * NPAIR].rearrange("p (h c) -> p h c", h=H)
            best = PP[:, 800:928].rearrange("p (h k) -> p h k", h=H)
            bpos = PP[:, 928:1056].bitcast(U32).rearrange("p (h k) -> p h k", h=H)
            bposf = T1[:, 0:P].rearrange("p (h k) -> p h k", h=H)
            ef = T1[:, P:2 * P]
            gd = T1[:, 2 * P:3 * P]

            def top16(src, n, width, value, index):
                for half in range(2):
                    lo, hi = 8 * half, 8 * half + 8
                    settle()
                    for l in range(n):
                        e.max(value[:, l, lo:hi], src(l)).then_inc(dve_done, c.count())
                    yield
                    settle()
                    for l in range(n):
                        e.max_index(index[:, l, lo:hi], value[:, l, lo:hi], src(l)).then_inc(dve_done, c.count())
                    if half == 0:
                        yield
                        settle()
                        for l in range(n):
                            e.match_replace(src(l), value[:, l, lo:hi], src(l), NEG).then_inc(dve_done, c.count())

            def score_at(l):
                h, p = l // 2, l % 2
                return 1024 * (h // 4) + 512 * p + P * (h % 4)

            def top1(st, T):
                e.wait_ge(act_done, c.at("act", "sc1"))
                yield from top16(lambda l: proj[:, score_at(l):score_at(l) + P], NL, P, val, ival)

            def top2(st, T):
                e.wait_ge(dve_done, c.here())
                e.tensor_copy(B1[:, 512:768], B1[:, 256:512].bitcast(U32)).then_inc(dve_done, c.count())
                e.wait_ge(dve_done, c.here())
                ts(fval[:, :, 0, :], fval[:, :, 0, :], 128.0, None, ALU.mult).then_inc(dve_done, c.count())
                e.wait_ge(dve_done, c.here())
                for src, dst in ((valp, cnd), (fval, cnde)):
                    at = 0
                    for a in range(8):
                        w = TOPK // (a + 1)
                        tt(dst[:, :, at:at + w], src[:, :, 0, a:a + 1].to_broadcast([P, H, w]),
                                 src[:, :, 1, 0:w], ALU.add).then_inc(dve_done, c.count())
                        at += w
                    tt(dst[:, :, at:at + 8], src[:, :, 0, 8:16], src[:, :, 1, 0:1].to_broadcast([P, H, 8]),
                             ALU.add).then_inc(dve_done, c.count())
                yield from top16(lambda l: cnd[:, l, :], H, NPAIR, best, bpos)

            def top3(st, T):
                e.wait_ge(dve_done, c.here())
                tt(gd.rearrange("p (h k) -> p h k", h=H), best, best[:, :, 0:1].to_broadcast([P, H, TOPK]),
                         ALU.subtract).then_inc(dve_done, c.count("best - max"))
                e.tensor_copy(T1[:, 0:P], PP[:, 928:1056].bitcast(U32)).then_inc(dve_done, c.count())
                eq = proj[:, 0:2 * TOPK * NPAIR].rearrange("p (k c) -> p k c", c=NPAIR)
                for q in range(4):
                    yield
                    for r in range(2):
                        h = 2 * q + r
                        v = eq[:, TOPK * r:TOPK * r + TOPK, :]
                        e.wait_ge(dve_done, c.here())
                        tt(v, bposf[:, h, :].unsqueeze(2).to_broadcast([P, TOPK, NPAIR]),
                                 iota[:].unsqueeze(1).to_broadcast([P, TOPK, NPAIR]), ALU.is_equal).then_inc(dve_done, c.count())
                        e.wait_ge(dve_done, c.here())
                        tt(v, v, cnde[:, h, :].unsqueeze(1).to_broadcast([P, TOPK, NPAIR]), ALU.mult).then_inc(dve_done, c.count())
                    e.wait_ge(dve_done, c.here())
                    red(ef[:, 32 * q:32 * q + 32], eq, AX, ALU.add).then_inc(dve_done, c.count())
                e.wait_ge(dve_done, c.here())
                e.tensor_copy(idx_a[:], ef).then_inc(dve_done, c.count())
                e.wait_ge(act_done, c.at("act", "gate exp"))
                gv = gd.rearrange("p (h k) -> p h k", h=H)
                red(small[:, 30:38], gv, AX, ALU.add).then_inc(dve_done, c.count())
                e.wait_ge(dve_done, c.here())
                e.reciprocal(small[:, 30:38], small[:, 30:38]).then_inc(dve_done, c.count())
                e.wait_ge(dve_done, c.here())
                tt(gate_a[:].rearrange("p (h k) -> p h k", h=H), gv,
                         small[:, 30:38].unsqueeze(2).to_broadcast([P, H, TOPK]), ALU.mult).then_inc(dve_done, c.count())

            def peer(st, T, s):
                n, g, j = nslots(st), s // GRP, s % GRP
                if s < n:
                    if j == 0 and g >= 2:
                        e.wait_ge(act_done, c.at("act", f"gelu{g - 2}"))
                    ring = f"gu{s % RING}"
                    e.wait_ge(S[ring], c.at(ring, f"u{s}") if s >= RING else c.begun(ring))
                    e.tensor_tensor_reduce(U[:, s % RING, :], U[:, s % RING, :], hr[:], 1.0, 0.0, ALU.mult, ALU.add,
                                           dots[:, g % 2, j:j + 1]).then_inc(dve_done, c.count(f"u{s}"))
                if s == n and st != "last":
                    e.wait_ge(dve_done, c.here())
                    e.tensor_copy(idx_u[:], idx_a[:]).then_inc(dve_done, c.count("idx_u"))
                s -= GRP
                if s >= 0:
                    if j == 0:
                        e.wait_ge(act_done, c.at("act", f"gelu{g - 1}"))
                    if s >= RING:
                        e.wait_ge(pe_done, c.at("pe", f"v{s - RING}"))
                    m = (fold if st == "second" else ident)[:]
                    ts(diag[:, s % RING, :], m, acts[:, (g - 1) % 2, j:j + 1], gate_r[:, s:s + 1], ALU.mult,
                       ALU.mult).then_inc(dve_done, c.count(f"d{s}"))

            def tail(st, T):
                if st != "first":
                    e.wait_ge(pe_done, c.at("pe", f"v{nslots(st) - 1}"))
                    e.wait_ge(act_done, c.at("act", "xr"))
                    tt(xr[:], Y, xr[:], ALU.add).then_inc(dve_done, c.count("y sum"))
                    if st != "last":
                        e.tensor_copy(idx_v[:], idx_a[:]).then_inc(dve_done, c.count())
                        e.tensor_copy(gate_r[:], gate_a[:]).then_inc(dve_done, c.count())
                    e.wait_ge(act_done, c.at("act", "y sq"))
                    invert(peerv[:, 1:2])
                    e.wait_ge(pe_done, c.at("pe", "gfin"))
                    e.wait_ge(dve_done, c.here())
                    stt(xr[:], xr[:], peerv[:, 1:2], Y, ALU.mult, ALU.mult).then_inc(dve_done, c.count("y"))
                else:
                    e.wait_ge(dve_done, c.here())
                    for src, dst in ((idx_a, idx_v), (gate_a, gate_r), (idx_a, idx_u)):
                        for lo in (0, 64):
                            e.tensor_copy(dst[lo:lo + 64, 0:64], src[lo:lo + 64, lo:lo + 64]).then_inc(
                                dve_done, c.count("idx_u" if dst is idx_u and lo else None))

            run(c, dict(norm1=norm1, kv=kv, ret1=ret1, ret2=ret2, q1=q1, att=att, out=out, norm2=norm2, top1=top1,
                        top2=top2, top3=top3, attend=attend), peer, tail, e)

    return new_counts, new_marks


def _apart(dm):
    return np.ascontiguousarray(dm[:, [0, 2, 4, 6, 1, 3, 5, 7], :])


def shape_constants():
    f = np.float32
    r = np.arange(P)
    pos = np.zeros((NTILE + 1, P))
    pos[0, 0:NSMP] = PAGES * P + np.arange(NSMP) % DEC_T
    pos[0, NSMP:NSMP + N_META] = np.arange(N_META)
    for t in range(1, NTILE + 1):
        pos[t] = N_META + (t - 1) * P + r
    inv = (f(10000.0) ** (-np.arange(32, dtype=f) / f(32))).astype(f)
    ang = (pos.astype(f)[:, :, None] * inv).astype(f)
    trig = np.concatenate([np.cos(ang), np.sin(ang)], axis=2).reshape(-1, 64).astype(f)
    lg = np.log(1.0 - 2.0 ** (-5.0 - np.arange(H)))

    def tables(start, length):
        i = r - start
        rel = r[None, :] - r[:, None]
        ok = (rel >= 0) & (start[None, :] == start[:, None]) & (length[None, :] > 0)
        d = np.exp(lg[:, None, None] * np.maximum(rel, 0)) * ok / 8.0
        dm = d.transpose(1, 0, 2).astype(f)
        cross = np.exp(lg[None, :] * (i[:, None] + 1.0))
        kdec = np.exp(lg[None, :] * (length[:, None] - 1.0 - i[:, None])) / 8.0 * (length[:, None] > 0)
        return dm, cross, kdec

    out = {}
    for n in range(2):
        if n == 0:
            start = np.where(r < NSMP, r // DEC_T * DEC_T, NSMP)
            length = np.where(r < NSMP, DEC_T, np.where(r < NSMP + N_META, N_META, 0))
            chunk = DEC_T
        else:
            start, length, chunk = np.zeros(P, int), np.full(P, P), P
        dm, cross, kdec = tables(start, length)
        one = np.zeros((P, 9))
        for b in range(DEC_B):
            one[DEC_T * b:DEC_T * b + DEC_T, b] = 1
        one[NSMP:NSMP + N_META, DEC_B] = 1
        gch = np.exp(lg[2 * np.arange(4)[None, :] + (r[:, None] >= 64)] * chunk)
        out[f"c_dmat{n}"] = _apart(dm)
        out[f"c_row{n}"] = np.concatenate([one, cross, kdec, gch], axis=1).astype(f)
    mask = np.full((NTILE + 1, P, NKEY), NEG, f)
    mask[:, :, SEQ + NSMP:SEQ + NSMP + N_META] = 0
    for t in range(1, NTILE + 1):
        mask[t, :, 0:SEQ][np.arange(SEQ)[None, :] <= (t - 1) * P + r[:, None]] = 0
    upper = lambda x: (np.ascontiguousarray(x, dtype=f).view(np.uint32) >> 16).astype(np.uint16)
    new = np.full((64, 248), NEG, f)
    for row in range(64):
        new[row, 120:121 + row // H] = 0
    out.update(c_ident=np.eye(P, dtype=f), c_trig=trig,
               c_fold=(r[:, None] % 64 == r[None, :] % 64).astype(f),
               c_iota=np.broadcast_to(np.arange(NPAIR, dtype=f), (P, NPAIR)).copy(),
               c_mask=upper(mask.reshape(-1, NKEY)), c_new=upper(new))
    return out


_INS = ["x_prompt", "x_sample", "cache_ckv", "cache_krope", "state_ret", "page_table", "meta_tokens", "w_in", "w_uq", "g_kv", "w_uv", "w_out", "g_ffn", "w_query", "u_experts", "v_experts", "g_final"]
_OUTS = dict(o_yp=(SEQ, D), o_ys=(NSMP, D), o_ckv_p=(SEQ + N_META, KV), o_kr_p=(SEQ + N_META, ROPE),
             o_ckv_s=(NSMP, KV), o_kr_s=(NSMP, ROPE), o_rp=(H, 64, 64), o_rs=(DEC_B, H, 64, 64))


def kernel(**inputs):
    import numpy as _np
    import concourse.bacc as _bacc
    from concourse import mybir as _mybir
    from concourse.bass_utils import run_bass_kernel_spmd as _run

    arrays = {n: _np.ascontiguousarray(inputs[n]) for n in _INS}
    arrays["t_uk"] = _np.ascontiguousarray(
        _np.asarray(inputs["w_uk"])[0].reshape(KV, 4, 2, NOPE).transpose(2, 3, 1, 0).reshape(P, 4, KV))
    arrays["t_keys"] = _np.ascontiguousarray(
        _np.asarray(inputs["sub_keys"])[0].transpose(1, 3, 0, 2).reshape(P, H, P))
    arrays["t_gcol"] = _np.ascontiguousarray(_np.concatenate(
        [_np.asarray(inputs["g_mix"]).reshape(NCH, P), _np.asarray(inputs["g_q"]).reshape(2, P)]).T)
    arrays.update(shape_constants())
    counts, marks = {}, {}
    for emission in range(2):
        nc = _bacc.Bacc("TRN2", target_bir_lowering=False, num_devices=1)
        args = {n: nc.dram_tensor(f"in_{n}", a.shape, _mybir.dt.from_np(a.dtype), kind="ExternalInput").ap()
                for n, a in arrays.items()}
        args.update({n: nc.dram_tensor(n, s, _mybir.dt.float32, kind="ExternalOutput").ap() for n, s in _OUTS.items()})
        counts, marks = build(nc, args, counts, marks)
    got = _run(nc, [{f"in_{n}": a for n, a in arrays.items()}], core_ids=[0]).results[0]
    return (got["o_yp"].reshape(1, SEQ, D), got["o_ys"].reshape(DEC_B, DEC_T, D),
            got["o_ckv_p"].reshape(1, 1, SEQ + N_META, KV), got["o_kr_p"].reshape(1, 1, SEQ + N_META, ROPE),
            got["o_ckv_s"].reshape(1, DEC_B, DEC_T, KV), got["o_kr_s"].reshape(1, DEC_B, DEC_T, ROPE),
            got["o_rp"].reshape(1, 1, H, 64, 64), got["o_rs"].reshape(1, DEC_B, H, 64, 64))
```
